# Optimizing a Trainium2 kernel written in Bass

```python
import jax, jax.numpy as jnp
from jax import lax
import numpy as np
import math

D_MODEL = 1024
BATCH = 1
SEQ = 512
DEPTH = 2

GRID_W = 64
CTX_LEN = 256
Q_BLOCK = 128
ROPE_THETA = 10000.0
EPS = 1e-6
N_MOD = 6
MLA_HEADS = 8
MLA_NOPE = 64
MLA_ROPE = 32
MLA_V = 64
MLA_Q_RANK = 384
MLA_KV_RANK = 256
POOL_WINDOWS = (2, 4, 8, 16)
POOL_WIDTH = 512
POOL_GROUP = POOL_WIDTH // len(POOL_WINDOWS)
MIX0_IN = MLA_Q_RANK + MLA_KV_RANK + MLA_ROPE + POOL_WIDTH
MIX0_OUT = MLA_HEADS * MLA_V + POOL_WIDTH
GQA_HEADS = 8
GQA_KV_HEADS = 2
GQA_HEAD_DIM = 128
GQA_GROUP = GQA_HEADS // GQA_KV_HEADS
GQA_Q_W = GQA_HEADS * GQA_HEAD_DIM
GQA_KV_W = GQA_KV_HEADS * GQA_HEAD_DIM
D_FF = 2816
CONV_W = 3
N_EVEN = (DEPTH + 1) // 2
N_ODD = DEPTH // 2


def rms_norm(x, gain=None):
    xf = x.astype(jnp.float32)
    y = (xf * lax.rsqrt(jnp.mean(xf * xf, axis=-1, keepdims=True) + EPS)).astype(x.dtype)
    return y if gain is None else y * gain

def modulate(x, shift, scale):
    return rms_norm(x) * (1.0 + scale) + shift

def axial_rope_tables(n_tokens, rope_dim):
    rows = n_tokens // GRID_W
    row = jnp.repeat(jnp.arange(rows, dtype=jnp.float32), GRID_W)
    col = jnp.tile(jnp.arange(GRID_W, dtype=jnp.float32), rows)
    n_freq = rope_dim // 4
    freq = ROPE_THETA ** (-jnp.arange(n_freq, dtype=jnp.float32) / n_freq)
    ang = jnp.concatenate([row[:, None] * freq, col[:, None] * freq], axis=-1)
    return jnp.cos(ang), jnp.sin(ang)

def apply_rope(x, cos, sin):
    xr = x.reshape(x.shape[:-1] + (x.shape[-1] // 2, 2))
    x0, x1 = xr[..., 0], xr[..., 1]
    c = cos[None, :, None, :].astype(x.dtype)
    s = sin[None, :, None, :].astype(x.dtype)
    return jnp.stack([x0 * c - x1 * s, x0 * s + x1 * c], axis=-1).reshape(x.shape)

def attention(q, k, v):
    B, Nq, KV, G, Dh = q.shape
    blk = min(Q_BLOCK, Nq)
    qb = jnp.moveaxis(q.reshape(B, Nq // blk, blk, KV, G, Dh), 1, 0)
    scale = Dh ** -0.5

    def one_block(qi):
        s = jnp.einsum('bqhgd,bkhd->bhgqk', qi, k).astype(jnp.float32) * scale
        p = jax.nn.softmax(s, axis=-1).astype(v.dtype)
        return jnp.einsum('bhgqk,bkhd->bqhgd', p, v)

    o = lax.map(one_block, qb)
    return jnp.moveaxis(o, 0, 1).reshape(B, Nq, KV * G * v.shape[-1])

def multiscale_pool(p, w_pool, s_pool):
    B, T, C = p.shape
    cs = jnp.cumsum(p.astype(jnp.float32), axis=1)
    cs = jnp.concatenate([jnp.zeros((B, 1, C), jnp.float32), cs], axis=1)
    t = jnp.arange(T)
    outs = []
    for g, w in enumerate(POOL_WINDOWS):
        lo = jnp.clip(t - w // 2, 0, T)
        hi = jnp.clip(t - w // 2 + w, 0, T)
        csg = cs[:, :, g * POOL_GROUP:(g + 1) * POOL_GROUP]
        mean = (csg[:, hi] - csg[:, lo]) / (hi - lo).astype(jnp.float32)[None, :, None]
        d = mean.astype(p.dtype) - p[:, :, g * POOL_GROUP:(g + 1) * POOL_GROUP]
        outs.append(d @ w_pool[g])
    return jnp.concatenate(outs, axis=-1) * s_pool

def mla_q(cq, g_q, w_uq, cos, sin, rope):
    B, T, _ = cq.shape
    q = (rms_norm(cq, g_q) @ w_uq).reshape(B, T, MLA_HEADS, MLA_NOPE + MLA_ROPE)
    if rope:
        q = jnp.concatenate([q[..., :MLA_NOPE], apply_rope(q[..., MLA_NOPE:], cos, sin)], axis=-1)
    return q[:, :, :, None, :]

def mla_kv(ckv, kr, g_kv, w_uk, w_uv, cos, sin, rope):
    B, T, _ = ckv.shape
    ckv = rms_norm(ckv, g_kv)
    k_nope = (ckv @ w_uk).reshape(B, T, MLA_HEADS, MLA_NOPE)
    v = (ckv @ w_uv).reshape(B, T, MLA_HEADS, MLA_V)
    kr = kr[:, :, None, :]
    if rope:
        kr = apply_rope(kr, cos, sin)
    k = jnp.concatenate([k_nope, jnp.broadcast_to(kr, (B, T, MLA_HEADS, MLA_ROPE))], axis=-1)
    return k, v

def mla_pool_mixer(hc, hl, w_in, g_q, w_uq, g_kv, w_uk, w_uv, w_pool, s_pool, w_out, cos, sin, need_ctx):
    i_kv = MLA_Q_RANK
    i_kr = i_kv + MLA_KV_RANK
    i_p = i_kr + MLA_ROPE
    pl = hl @ w_in
    ql = mla_q(pl[..., :i_kv], g_q, w_uq, cos, sin, True)
    kl, vl = mla_kv(pl[..., i_kv:i_kr], pl[..., i_kr:i_p], g_kv, w_uk, w_uv, cos, sin, True)
    if need_ctx:
        pc = hc @ w_in
        qc = mla_q(pc[..., :i_kv], g_q, w_uq, cos, sin, False)
        kc, vc = mla_kv(pc[..., i_kv:i_kr], pc[..., i_kr:i_p], g_kv, w_uk, w_uv, cos, sin, False)
    else:
        pkv = hc @ w_in[:, i_kv:i_p]
        kc, vc = mla_kv(pkv[..., :MLA_KV_RANK], pkv[..., MLA_KV_RANK:], g_kv, w_uk, w_uv, cos, sin, False)
    al = attention(ql, jnp.concatenate([kc, kl], axis=1), jnp.concatenate([vc, vl], axis=1))
    ol = jnp.concatenate([al, multiscale_pool(pl[..., i_p:], w_pool, s_pool)], axis=-1) @ w_out
    oc = None
    if need_ctx:
        ac = attention(qc, kc, vc)
        oc = jnp.concatenate([ac, multiscale_pool(pc[..., i_p:], w_pool, s_pool)], axis=-1) @ w_out
    return oc, ol

def gqa_q(a, g_q, cos, sin, rope):
    B, T, _ = a.shape
    q = rms_norm(a.reshape(B, T, GQA_HEADS, GQA_HEAD_DIM), g_q)
    if rope:
        q = apply_rope(q, cos, sin)
    return q.reshape(B, T, GQA_KV_HEADS, GQA_GROUP, GQA_HEAD_DIM)

def gqa_kv(a, g_k, cos, sin, rope):
    B, T, _ = a.shape
    k = rms_norm(a[..., :GQA_KV_W].reshape(B, T, GQA_KV_HEADS, GQA_HEAD_DIM), g_k)
    v = a[..., GQA_KV_W:].reshape(B, T, GQA_KV_HEADS, GQA_HEAD_DIM)
    if rope:
        k = apply_rope(k, cos, sin)
    return k, v

def gqa_mixer(hc, hl, w_in, g_q, g_k, w_out, cos, sin, need_ctx):
    pl = hl @ w_in
    ql = gqa_q(pl[..., :GQA_Q_W], g_q, cos, sin, True)
    kl, vl = gqa_kv(pl[..., GQA_Q_W:], g_k, cos, sin, True)
    if need_ctx:
        pc = hc @ w_in
        qc = gqa_q(pc[..., :GQA_Q_W], g_q, cos, sin, False)
        kc, vc = gqa_kv(pc[..., GQA_Q_W:], g_k, cos, sin, False)
    else:
        kc, vc = gqa_kv(hc @ w_in[:, GQA_Q_W:], g_k, cos, sin, False)
    ol = attention(ql, jnp.concatenate([kc, kl], axis=1), jnp.concatenate([vc, vl], axis=1)) @ w_out
    oc = attention(qc, kc, vc) @ w_out if need_ctx else None
    return oc, ol

def conv_ffn(h, w_up, conv_w, conv_b, w_down):
    a = h @ w_up
    g, u = a[..., :D_FF], a[..., D_FF:]
    T = g.shape[1]
    half = CONV_W // 2
    gp = jnp.pad(g, ((0, 0), (half, half), (0, 0)))
    acc = conv_b + gp[:, 0:T] * conv_w[0]
    for j in range(1, CONV_W):
        acc = acc + gp[:, j:j + T] * conv_w[j]
    return (jax.nn.silu(acc) * u) @ w_down

def first_inputs(seed: int = 0) -> dict:
    key = jax.random.key(seed)
    ks = iter(jax.random.split(key, 32))
    D = D_MODEL

    def normal(shape, scale=1.0):
        return jax.random.normal(next(ks), shape, jnp.float32) * scale

    def gain(shape):
        return 1.0 + 0.05 * normal(shape)

    return {
        'x': normal((BATCH, SEQ, D)),
        'c': normal((BATCH, D)),
        'ctx': normal((BATCH, CTX_LEN, D)),
        'c_ctx': normal((D,)),
        'w_mod': normal((DEPTH, D, N_MOD * D), D ** -0.5),
        'b_mod': normal((DEPTH, N_MOD * D), 0.02),
        'mix0_w_in': normal((N_EVEN, D, MIX0_IN), D ** -0.5),
        'mla_g_q': gain((N_EVEN, MLA_Q_RANK)),
        'mla_w_uq': normal((N_EVEN, MLA_Q_RANK, MLA_HEADS * (MLA_NOPE + MLA_ROPE)), MLA_Q_RANK ** -0.5),
        'mla_g_kv': gain((N_EVEN, MLA_KV_RANK)),
        'mla_w_uk': normal((N_EVEN, MLA_KV_RANK, MLA_HEADS * MLA_NOPE), MLA_KV_RANK ** -0.5),
        'mla_w_uv': normal((N_EVEN, MLA_KV_RANK, MLA_HEADS * MLA_V), MLA_KV_RANK ** -0.5),
        'pool_w': normal((N_EVEN, len(POOL_WINDOWS), POOL_GROUP, POOL_GROUP), POOL_GROUP ** -0.5),
        'pool_scale': gain((N_EVEN, POOL_WIDTH)),
        'mix0_w_out': normal((N_EVEN, MIX0_OUT, D), MIX0_OUT ** -0.5),
        'gqa_w_in': normal((N_ODD, D, GQA_Q_W + 2 * GQA_KV_W), D ** -0.5),
        'gqa_g_q': gain((N_ODD, GQA_HEAD_DIM)),
        'gqa_g_k': gain((N_ODD, GQA_HEAD_DIM)),
        'gqa_w_out': normal((N_ODD, GQA_Q_W, D), GQA_Q_W ** -0.5),
        'ffn_w_up': normal((DEPTH, D, 2 * D_FF), D ** -0.5),
        'ffn_conv_w': normal((DEPTH, CONV_W, D_FF), CONV_W ** -0.5),
        'ffn_conv_b': normal((DEPTH, D_FF), 0.02),
        'ffn_w_down': normal((DEPTH, D_FF, D), D_FF ** -0.5),
        'g_final': gain((D,)),
    }

def first_block(x, c, ctx, c_ctx, w_mod, b_mod, mix0_w_in, mla_g_q, mla_w_uq, mla_g_kv, mla_w_uk, mla_w_uv,
              pool_w, pool_scale, mix0_w_out, gqa_w_in, gqa_g_q, gqa_g_k, gqa_w_out,
              ffn_w_up, ffn_conv_w, ffn_conv_b, ffn_w_down, g_final):
    B, N, D = x.shape
    cos_a, sin_a = axial_rope_tables(N, MLA_ROPE)
    cos_c, sin_c = axial_rope_tables(N, GQA_HEAD_DIM)
    xl, xc = x, ctx
    for i in range(DEPTH):
        last = i == DEPTH - 1
        j = i // 2
        ml = (jax.nn.silu(c) @ w_mod[i] + b_mod[i]).reshape(B, N_MOD, 1, D)
        mc = (jax.nn.silu(c_ctx) @ w_mod[i] + b_mod[i]).reshape(N_MOD, D)
        hl = modulate(xl, ml[:, 0], ml[:, 1])
        hc = modulate(xc, mc[0], mc[1])
        if i % 2 == 0:
            oc, ol = mla_pool_mixer(hc, hl, mix0_w_in[j], mla_g_q[j], mla_w_uq[j], mla_g_kv[j], mla_w_uk[j],
                                    mla_w_uv[j], pool_w[j], pool_scale[j], mix0_w_out[j], cos_a, sin_a, not last)
        else:
            oc, ol = gqa_mixer(hc, hl, gqa_w_in[j], gqa_g_q[j], gqa_g_k[j], gqa_w_out[j], cos_c, sin_c, not last)
        xl = xl + ml[:, 2] * ol
        xl = xl + ml[:, 5] * conv_ffn(modulate(xl, ml[:, 3], ml[:, 4]),
                                      ffn_w_up[i], ffn_conv_w[i], ffn_conv_b[i], ffn_w_down[i])
        if not last:
            xc = xc + mc[2] * oc
            xc = xc + mc[5] * conv_ffn(modulate(xc, mc[3], mc[4]),
                                       ffn_w_up[i], ffn_conv_w[i], ffn_conv_b[i], ffn_w_down[i])
    return rms_norm(xl, g_final)


N_MIXERS = 2

A_EXPAND = 2
A_WIDTH = A_EXPAND * D_MODEL
A_CHUNK = 128
A_HEADS = 16
A_HEAD_DIM = A_WIDTH // A_HEADS

B_GROUPS = ((128, 1), (512, 4), (2048, 16))
B_N_GROUPS = len(B_GROUPS)
B_HEADS = 16
B_HEAD_DIM = 64
B_WIDTH = B_HEADS * B_HEAD_DIM
B_QKV = B_N_GROUPS * 3 * B_WIDTH
B_TOTAL_HEADS = B_N_GROUPS * B_HEADS

REL_BUCKETS = 32
REL_EXACT = 8
REL_MAX_DISTANCE = 1024

N_A_LAYERS = (DEPTH + 1) // 2
N_B_LAYERS = DEPTH // 2
NEG_INF = -1e30


def rms_norm_2(x, g):
    xf = x.astype(jnp.float32)
    y = xf * lax.rsqrt(jnp.mean(xf * xf, axis=-1, keepdims=True) + EPS)
    return (y * g.astype(jnp.float32)).astype(x.dtype)

def layer_norm(x, g, b):
    xf = x.astype(jnp.float32)
    mu = jnp.mean(xf, axis=-1, keepdims=True)
    xc = xf - mu
    y = xc * lax.rsqrt(jnp.mean(xc * xc, axis=-1, keepdims=True) + EPS)
    return (y * g.astype(jnp.float32) + b.astype(jnp.float32)).astype(x.dtype)

def t5_bucket(rel):
    half = REL_BUCKETS // 2
    ret = jnp.where(rel > 0, half, 0)
    n = jnp.abs(rel)
    nf = jnp.maximum(n, 1).astype(jnp.float32)
    large = REL_EXACT + (jnp.log(nf / REL_EXACT) / math.log(REL_MAX_DISTANCE / REL_EXACT)
                         * (half - REL_EXACT)).astype(jnp.int32)
    large = jnp.minimum(large, half - 1)
    return ret + jnp.where(n < REL_EXACT, n, large)

def gmlp_mixer(h, w_in, w_s, b_s, vn_g, vn_b, w_out):
    bsz, s, _ = h.shape
    z = h @ w_in
    u, v, g = jnp.split(z, 3, axis=-1)
    u = jax.nn.gelu(u)
    v = layer_norm(jax.nn.gelu(v), vn_g, vn_b)
    nc = s // A_CHUNK
    vc = v.reshape(bsz, nc, A_CHUNK, A_HEADS, A_HEAD_DIM)
    sg = jnp.einsum('hpq,bcqhd->bcphd', w_s, vc) + b_s.T[None, None, :, :, None]
    y = u * sg.reshape(bsz, s, A_WIDTH) * jax.nn.silu(g)
    return y @ w_out

def dilated_window_group(q, k, v, table, dilation, half_w):
    bsz, s, nh, dh = q.shape
    L = s // dilation
    W = half_w
    nb = -(-L // W)
    Lp = nb * W

    def strided(t):
        return t.reshape(bsz, L, dilation, nh, dh).transpose(0, 2, 1, 3, 4)

    qs = jnp.pad(strided(q), ((0, 0), (0, 0), (0, Lp - L), (0, 0), (0, 0)))
    pad_kv = ((0, 0), (0, 0), (W, Lp - L + W), (0, 0), (0, 0))
    kp = jnp.pad(strided(k), pad_kv).reshape(bsz, dilation, nb + 2, W, nh, dh)
    vp = jnp.pad(strided(v), pad_kv).reshape(bsz, dilation, nb + 2, W, nh, dh)

    def band(t):
        return jnp.concatenate([t[:, :, 0:nb], t[:, :, 1:nb + 1], t[:, :, 2:nb + 2]], axis=3)

    kb, vb = band(kp), band(vp)
    qb = qs.reshape(bsz, dilation, nb, W, nh, dh)

    logits = jnp.einsum('bnkqhd,bnkjhd->bnkhqj', qb, kb,
                        preferred_element_type=jnp.float32) * (dh ** -0.5)
    qi = jnp.arange(W, dtype=jnp.int32)[:, None]
    kj = jnp.arange(3 * W, dtype=jnp.int32)[None, :]
    rel = kj - W - qi
    bias = table.astype(jnp.float32)[t5_bucket(rel * dilation)].transpose(2, 0, 1)
    key_pos = jnp.arange(nb, dtype=jnp.int32)[:, None] * W + kj - W
    mask = (jnp.abs(rel) <= W)[None] & ((key_pos >= 0) & (key_pos < L))[:, None, :]
    logits = jnp.where(mask[None, None, :, None], logits + bias, NEG_INF)

    m = jnp.max(logits, axis=-1, keepdims=True)
    p = jnp.exp(logits - m)
    den = jnp.sum(p, axis=-1, keepdims=True)
    o = jnp.einsum('bnkhqj,bnkjhd->bnkqhd', p / den, vb.astype(jnp.float32))
    lse = (m + jnp.log(den))[..., 0]

    o = o.reshape(bsz, dilation, Lp, nh, dh)[:, :, :L].transpose(0, 2, 1, 3, 4).reshape(bsz, s, nh, dh)
    lse = lse.transpose(0, 1, 2, 4, 3).reshape(bsz, dilation, Lp, nh)[:, :, :L]
    lse = lse.transpose(0, 2, 1, 3).reshape(bsz, s, nh)
    return o, lse

def dilated_attention_mixer(h, w_in, w_out, rel_table):
    bsz, s, _ = h.shape
    z = h @ w_in
    qkv = z[..., :B_QKV].reshape(bsz, s, B_N_GROUPS, 3, B_HEADS, B_HEAD_DIM)
    gate = z[..., B_QKV:]
    outs, lses = [], []
    for gi, (window, dil) in enumerate(B_GROUPS):
        o, lse = dilated_window_group(qkv[:, :, gi, 0], qkv[:, :, gi, 1], qkv[:, :, gi, 2],
                                      rel_table[:, gi * B_HEADS:(gi + 1) * B_HEADS],
                                      dil, window // (2 * dil))
        outs.append(o)
        lses.append(lse)
    wts = jax.nn.softmax(jnp.stack(lses), axis=0)
    o = jnp.einsum('gbsh,gbshd->bshd', wts, jnp.stack(outs))
    y = o.reshape(bsz, s, B_WIDTH).astype(h.dtype) * jax.nn.silu(gate)
    return y @ w_out

def second_inputs(seed: int = 0) -> dict:
    key = jax.random.key(seed)
    ks = jax.random.split(key, 16)
    f32 = jnp.float32
    x = jax.random.normal(ks[0], (BATCH, SEQ, D_MODEL), f32)
    norm_pre = 1.0 + 0.1 * jax.random.normal(ks[1], (DEPTH, D_MODEL), f32)
    norm_post = 1.0 + 0.1 * jax.random.normal(ks[2], (DEPTH, D_MODEL), f32)
    a_w_in = jax.random.normal(ks[3], (N_A_LAYERS, D_MODEL, 3 * A_WIDTH), f32) * D_MODEL ** -0.5
    a_w_s = jax.random.normal(ks[4], (N_A_LAYERS, A_HEADS, A_CHUNK, A_CHUNK), f32) * A_CHUNK ** -0.5
    a_b_s = 1.0 + 0.1 * jax.random.normal(ks[5], (N_A_LAYERS, A_HEADS, A_CHUNK), f32)
    a_vnorm_g = 1.0 + 0.1 * jax.random.normal(ks[6], (N_A_LAYERS, A_WIDTH), f32)
    a_vnorm_b = 0.1 * jax.random.normal(ks[7], (N_A_LAYERS, A_WIDTH), f32)
    a_w_out = jax.random.normal(ks[8], (N_A_LAYERS, A_WIDTH, D_MODEL), f32) * A_WIDTH ** -0.5
    b_w_in = jax.random.normal(ks[9], (N_B_LAYERS, D_MODEL, B_QKV + B_WIDTH), f32) * D_MODEL ** -0.5
    b_w_out = jax.random.normal(ks[10], (N_B_LAYERS, B_WIDTH, D_MODEL), f32) * B_WIDTH ** -0.5
    rel_bias = 0.5 * jax.random.normal(ks[11], (REL_BUCKETS, B_TOTAL_HEADS), f32)
    return {"x": x, "norm_pre": norm_pre, "norm_post": norm_post,
            "a_w_in": a_w_in, "a_w_s": a_w_s, "a_b_s": a_b_s,
            "a_vnorm_g": a_vnorm_g, "a_vnorm_b": a_vnorm_b, "a_w_out": a_w_out,
            "b_w_in": b_w_in, "b_w_out": b_w_out, "rel_bias": rel_bias}

def second_block(x, norm_pre, norm_post, a_w_in, a_w_s, a_b_s, a_vnorm_g, a_vnorm_b, a_w_out,
              b_w_in, b_w_out, rel_bias):
    for i in range(DEPTH):
        h = rms_norm_2(x, norm_pre[i])
        j = i // N_MIXERS
        if i % N_MIXERS == 0:
            y = gmlp_mixer(h, a_w_in[j], a_w_s[j], a_b_s[j], a_vnorm_g[j], a_vnorm_b[j], a_w_out[j])
        else:
            y = dilated_attention_mixer(h, b_w_in[j], b_w_out[j], rel_bias)
        x = x + rms_norm_2(y, norm_post[i])
    return x


def setup_inputs(seed=0):
    out = dict(first_inputs(seed))
    for name, value in second_inputs(seed + 1).items():
        if name != "x":
            out[name + "_2"] = value
    return out


def reference(
    x, c, ctx, c_ctx, w_mod, b_mod, mix0_w_in, mla_g_q, mla_w_uq, mla_g_kv, mla_w_uk, mla_w_uv,
    pool_w, pool_scale, mix0_w_out, gqa_w_in, gqa_g_q, gqa_g_k, gqa_w_out, ffn_w_up, ffn_conv_w,
    ffn_conv_b, ffn_w_down, g_final, norm_pre_2, norm_post_2, a_w_in_2, a_w_s_2, a_b_s_2,
    a_vnorm_g_2, a_vnorm_b_2, a_w_out_2, b_w_in_2, b_w_out_2, rel_bias_2,
):
    x = first_block(
        x, c, ctx, c_ctx, w_mod, b_mod, mix0_w_in, mla_g_q, mla_w_uq, mla_g_kv, mla_w_uk,
        mla_w_uv, pool_w, pool_scale, mix0_w_out, gqa_w_in, gqa_g_q, gqa_g_k, gqa_w_out,
        ffn_w_up, ffn_conv_w, ffn_conv_b, ffn_w_down, g_final,
    )
    return second_block(
        x, norm_pre_2, norm_post_2, a_w_in_2, a_w_s_2, a_b_s_2, a_vnorm_g_2, a_vnorm_b_2,
        a_w_out_2, b_w_in_2, b_w_out_2, rel_bias_2,
    )


_drawn_inputs = setup_inputs


def setup_inputs(seed=0):
    import zlib

    import numpy as np

    out = dict(_drawn_inputs(seed))
    spreads = {}
    factors = {'mla_g_q': 8.0, 'mla_g_kv': 2.776, 'gqa_g_q': 8.0, 'gqa_g_k': 8.0, 'ffn_conv_b': 2.861}
    for name, (base, spread) in spreads.items():
        noise = np.random.default_rng([zlib.crc32(name.encode()), seed]).standard_normal(out[name].shape)
        drawn = base * np.exp(spread * noise) if base else spread * noise
        out[name] = __import__('jax').numpy.asarray(drawn.astype(out[name].dtype))
    for name, factor in factors.items():
        out[name] = (out[name] * factor).astype(out[name].dtype)
    return out
```

```python
from contextlib import ExitStack

import numpy as np

import concourse.bass as bass
from concourse import mybir

F32 = mybir.dt.float32
F32R = mybir.dt.float32r
ALU = mybir.AluOpType
ACT = mybir.ActivationFunctionType
AX = mybir.AxisListType

P = 128
D = 1024
KC = D // P
TM, TC = 512, 256
TA = TM + TC
GRID_W = 64
EPS = 1e-6
Q_RANK, KV_RANK, ROPE_A, NOPE, POOL_W = 384, 256, 32, 64, 512
DH_A = NOPE + ROPE_A
FF = 2816
FC = FF // P
WINDOWS = (2, 4, 8, 16)
PAD = 8
PLEN = PAD + TC + 2 * PAD + TM + PAD
A_HEADS = 16
B_HEADS = 16
DILATIONS, HALF_W = (1, 4, 16), 64
BUCKETS = 32
NDELTA = 7
NREL = NDELTA + 2
TW = 2 * P
NEG = -1e30
GROUP = 4

TILES = {}
_at = 0
for _name, _n in (("pool_in", 4), ("cq_in", 3), ("ckv_in", 2), ("kr_in", 1), ("pool_w", 1), ("mla", 8),
                  ("mix_out", 8), ("ffn0", 2 * FC + 20 + 2), ("gqa_kv", 4), ("gqa_q", 8), ("gqa_out", 8),
                  ("ffn1", 2 * FC + 20 + 2), ("ws", 2), ("gmlp_v", 16), ("gmlp", 4 * 12), ("dil", 80), ("dil_out", 8)):
    TILES[_name] = _at
    _at += _n
N_TILES = _at

COL = {}
_at = 0
for _name, _n in (("b_mod", 96), ("g_q", 3), ("g_kv", 2), ("s_pool", 4), ("gq", 1), ("gk", 1),
                  ("conv0", 4 * FC), ("conv1", 4 * FC), ("g_final", 8), ("pre0", 8), ("pre1", 8),
                  ("post0", 8), ("post1", 8)):
    COL[_name] = _at
    _at += _n
N_COLS = _at


class At:

    def __init__(self, start, step=0, i=None, nth=0):
        self.start, self.step, self.i, self.nth = start, step if i is not None else 0, i, nth

    def __add__(self, k):
        return At(self.start + k, self.step, self.i, self.nth + k)

    def __sub__(self, k):
        return self + -k

    def times(self, m=1, plus=0):
        v = m * self.start + plus
        return v if self.i is None or m * self.step == 0 else self.i * (m * self.step) + v

    def mod(self, n):
        assert self.step % n == 0
        return self.start % n

    def over(self, n):
        assert self.step % n == 0
        return At(self.start // n, self.step // n, self.i)

    def ds(self, n=1, scale=1, plus=0):
        return bass.ds(self.times(scale, plus), n)


def build(nc, a, out):
    FIRST_MODS, MLA_MODS, OUT_MODS, FFN_MODS = 16, 8, 4, 2

    def at_bytes(name, shape, off, dt=F32):
        return nc.alloc_sbuf_tensor_at(name, shape, dt, offset=off)

    base = -(-nc.sbuf_base // 64) * 64
    cur = [base]

    def keep(name, shape, dt=F32):
        t = at_bytes(name, shape, cur[0], dt)
        cur[0] += -(-int(np.prod(shape[1:])) * 4 // 32) * 32
        return t

    X_M = keep("X_M", [P, KC, TM])
    x_c_at = cur[0]
    X_C = keep("X_C", [P, KC, TC])
    RAW = keep("RAW", [P, 2, D])
    WH = keep("WH", [P, 2, D], F32R)
    WL = keep("WL", [P, 2, D], F32R)
    mraw_at = cur[0]
    MRAW = keep("MRAW", [P, 2, D])
    MOD = keep("MOD", [P, 96, 2])
    COLS = keep("COLS", [P, N_COLS])
    CVEC = keep("CVEC", [P, KC, 2])
    ONES = keep("ONES", [P, P])
    IDENT = keep("IDENT", [P, P])
    SCALE1 = keep("SCALE1", [P, KC, 2])
    CONST = keep("CONST", [P, 32])
    STAT = keep("STAT", [P, 2, 8])
    LN = keep("LN", [P, 4, 24])
    scratch = cur[0]
    RB = keep("RB", [P, TA])
    SQ = keep("SQ", [P, 2, TA])
    T = keep("T", [P, 2, TA])
    arena = cur[0]

    def place(name, shape, off, dt=F32):
        return at_bytes(name, shape, arena + off, dt)

    KB = 1024
    HM = [place(f"HM{n}", [P, KC, TM], n * 16 * KB, F32R) for n in range(2)]
    HC = [place(f"HC{n}", [P, KC, TC], (32 + n * 8) * KB, F32R) for n in range(2)]
    GM = [place(f"GM{n}", [P, KC, TM], (48 + n * 16) * KB, F32R) for n in range(2)]
    GC = [place(f"GC{n}", [P, KC, TC], (80 + n * 8) * KB, F32R) for n in range(2)]
    top = 96 * KB
    LAT = place("LAT", [P, 6, TA], top)
    PB = [place(f"PB{n}", [P, PLEN], top + 6 * TA * 4 + n * PLEN * 4) for n in range(3)]
    EDGE = place("EDGE", [P, 4, 4, PAD], top + 6 * TA * 4 + 3 * PLEN * 4)
    ONEHOT = place("ONEHOT", [BUCKETS, NREL * TW], 48 * KB)
    RELMASK = place("RELMASK", [B_HEADS, NREL * TW], 60 * KB)
    BVEC = place("BVEC", [B_HEADS, NREL * TW], top + 6 * TA * 4 + 3 * PLEN * 4 + 4 * 4 * PAD * 4)
    REL = place("REL", [BUCKETS, 48], 84 * KB)
    CQ = [place(f"CQ{n}", [P, 3, TA], n * 9 * KB, F32R) for n in range(2)]
    CKV = [place(f"CKV{n}", [P, 2, TA], (18 + n * 6) * KB, F32R) for n in range(2)]
    KA = [place(f"KA{n}", [P, 2, TA], (30 + n * 6) * KB, F32R) for n in range(2)]
    VA = [place(f"VA{n}", [P, 6, P], (42 + n * 3) * KB, F32R) for n in range(2)]
    QA = [place(f"QA{n}", [P, 2, TA], (96 + n * 6) * KB, F32R) for n in range(2)]
    PTA = [place(f"PTA{n}", [P, 2, 6, 2 * P], (108 + n * 12) * KB, F32R) for n in range(2)]
    sq_at, t_at = scratch + TA * 4, scratch + 3 * TA * 4
    ROPE_TA = at_bytes("ROPE_TA", [P, 2, TM], sq_at)
    PROB = at_bytes("PROB", [P, 2, TA], t_at)
    PROB4 = at_bytes("PROB4", [P, 4, TA], sq_at)
    RT = [at_bytes("RT0", [P, TM], sq_at + 4096), at_bytes("RT1", [P, TM], scratch)]
    MROW = place("MROW", [2, 2 * P], 132 * KB)
    KG = [place(f"KG{n}", [P, 2, TA], (80 + n * 6) * KB, F32R) for n in range(2)]
    VG = [place(f"VG{n}", [P, 6, 2, P], (96 + n * 6) * KB, F32R) for n in range(2)]
    PTG = PTA
    QG = [place(f"QG{n}", [P, 2, TM], (32 + n * 4) * KB, F32R) for n in range(2)]
    HEADN = at_bytes("HEADN", [P, 2, TA], mraw_at)
    ROPE_TG = at_bytes("ROPE_TG", [P, 2, TM], x_c_at)
    RG = [at_bytes(f"RG{n}", [P, TM], x_c_at + (4 + 2 * n) * KB) for n in range(2)]
    Y = place("Y", [P, KC, TM], 32 * KB)
    PG = [place(f"PG{n}", [P, 4, TM], (48 + n * 8) * KB, F32R) for n in range(2)]
    VN_GB = place("VN_GB", [P, 2, A_HEADS * P], 64 * KB)
    V = place("V", [P, 4, A_HEADS * P], 80 * KB)
    WS = [place(f"WS{n}", [P, A_HEADS * P], (112 + n * 8) * KB, F32R) for n in range(2)]
    UG, TH, GG, YG = [at_bytes(name, [P, TM], sq_at + 2 * n * KB) for n, name in enumerate(("UG", "TH", "GG", "YG"))]
    SQV = at_bytes("SQV", [P, A_HEADS * P], sq_at)
    BS = at_bytes("BS", [P, A_HEADS * P], x_c_at)
    VT = at_bytes("VT", [P, 4, P], mraw_at)
    VS = [at_bytes(f"VS{n}", [P, 4, P], mraw_at + (2 + 2 * n) * KB, F32R) for n in range(2)]
    SB = at_bytes("SB", [P, TM], mraw_at + 6 * KB)
    DG = [place(f"DG{n}", [P, KC, TM], (32 + n * 16) * KB, F32R) for n in range(2)]
    QD = [place(f"QD{n}", [P, 3, TM], (64 + n * 6) * KB, F32R) for n in range(2)]
    KD = [place(f"KD{n}", [P, 3, TM], (76 + n * 6) * KB, F32R) for n in range(2)]
    VD = [place(f"VD{n}", [P, 3, 4, P], (88 + n * 6) * KB, F32R) for n in range(2)]
    PTD = [place(f"PTD{n}", [P, 2, 6, 2 * P], (100 + n * 12) * KB, F32R) for n in range(2)]
    TB = place("TB", [P, 2, NREL, P], 124 * KB)
    YD = place("YD", [P, KC, TM], 64 * KB)
    VF = at_bytes("VF", [P, 3, TM], mraw_at)
    SILG = at_bytes("SILG", [P, TM], x_c_at)
    THG = at_bytes("THG", [P, TM], x_c_at + 2 * KB)
    OG = at_bytes("OG", [P, 2 * P], x_c_at + 4 * KB)
    CONV = place("CONV", [P, 2, TA], 96 * KB)
    GATED = place("GATED", [P, 2, TA], 102 * KB)

    dt_scratch = nc.dram_tensor("bias_rows", (B_HEADS, NREL * TW), F32, kind="Internal").ap()

    ctx = ExitStack()
    with ctx:
        PS = ctx.enter_context(nc.psum_tensor("PS", [P, 8, 512], F32))
        psf = PS[:, :, :].rearrange("p b n -> p (b n)")

        def sem(name):
            return ctx.enter_context(nc.semaphore(name))

        params_loaded = sem("params_loaded")
        x_loaded = sem("x_loaded")
        tile_loaded = [sem("tile_loaded0"), sem("tile_loaded1")]
        tile_hi = sem("tile_hi")
        tile_split = [sem("tile_split0"), sem("tile_split1")]
        mod_loaded = [sem("mod_loaded0"), sem("mod_loaded1")]
        mod_done = sem("mod_done")
        mod_row = sem("mod_row")
        mod_turned = sem("mod_turned")
        mod_read = sem("mod_read")
        silu_ready = sem("silu_ready")
        ones_ready = sem("ones_ready")
        acc_done = sem("acc_done")
        acc_read = sem("acc_read")
        sq_ready = sem("sq_ready")
        sq_used = sem("sq_used")
        rms_ready = sem("rms_ready")
        rb_ready = sem("rb_ready")
        norm_scaled = sem("norm_scaled")
        norm_hi = sem("norm_hi")
        norm_ready = sem("norm_ready")
        scale1_ready = sem("scale1_ready")
        pool_step = sem("pool_step")
        pool_hi = sem("pool_hi")
        pool_ready = sem("pool_ready")
        pad_zero = sem("pad_zero")
        poolout_hi = sem("poolout_hi")
        conv_center = sem("conv_center")
        conv_tap = sem("conv_tap")
        silu_done = sem("silu_done")
        gated_hi = sem("gated_hi")
        gated_ready = sem("gated_ready")
        stored = sem("stored")
        score_done = sem("score_done")
        score_free = [sem("score_free0"), sem("score_free1")]
        proj_hi = sem("proj_hi")
        rope_step = sem("rope_step")
        rope_done = sem("rope_done")
        max_ready = sem("max_ready")
        recip_ready = sem("recip_ready")
        prob_ready = sem("prob_ready")
        pt_done = sem("pt_done")
        pt_hi = sem("pt_hi")
        pt_ready = sem("pt_ready")
        o_done = sem("o_done")
        o_hi = sem("o_hi")
        o_read = sem("o_read")
        rope_loaded = sem("rope_loaded")
        rope_c_loaded = sem("rope_c_loaded")
        head_sq = sem("head_sq")
        head_sum = sem("head_sum")
        head_rms = sem("head_rms")
        head_inverse = sem("head_inverse")
        head_split = sem("head_split")
        x_ready = sem("x_ready")
        v_tile_done = sem("v_tile_done")
        rows_loaded = sem("rows_loaded")
        y_zero = sem("y_zero")
        mean_ready = sem("mean_ready")
        var_ready = sem("var_ready")
        std_ready = sem("std_ready")
        v_normed = sem("v_normed")
        v_step = sem("v_step")
        vs_hi = sem("vs_hi")
        vs_ready = sem("vs_ready")
        th_ready = sem("th_ready")
        gu_ready = sem("gu_ready")
        y_ready = sem("y_ready")
        gm_hi = sem("gm_hi")
        gm_ready = sem("gm_ready")
        post_scaled = sem("post_scaled")
        rel_loaded = sem("rel_loaded")
        bias_sum = sem("bias_sum")
        bias_ready = sem("bias_ready")
        bias_stored = sem("bias_stored")
        tb_loaded = [sem("tb_loaded0"), sem("tb_loaded1")]
        dil_hi = sem("dil_hi")
        vt_done = sem("vt_done")
        vt_read = sem("vt_read")
        thg_ready = sem("thg_ready")
        both_max = sem("both_max")
        exp_ready = sem("exp_ready")
        o_scaled = sem("o_scaled")
        kr_hi = sem("kr_hi")
        rope_used = sem("rope_used")
        edge_loaded = sem("edge_loaded")
        pool_diff = sem("pool_diff")

        block = ctx.enter_context(nc.Block())

        UNIT = {}
        u = 0
        for name, n in (("in", 10), ("pool_w", 4), ("mix_out", 8), ("ffn0", 2 * FC + 6 * KC), ("gqa_out", 8),
                        ("ffn1", 2 * FC + 6 * KC), ("gmlp_v", 16), ("gmlp", 4 * 20), ("dil_out", 8)):
            UNIT[name] = u
            u += n
        NORM = {}
        c = 0
        for n, (name, chunks) in enumerate((("mix0", 8), ("cq", 3), ("ckv", 2), ("ffn0", 8), ("mix1", 8), ("ffn1", 8),
                                            ("final", 8), ("gmlp", 8), ("gmlp_post", 8), ("dil", 8), ("dil_post", 8))):
            NORM[name] = (n, c)
            c += chunks
        SPLITS = {}
        c = 0
        for name, chunks in (("mix0", 8), ("cq", 3), ("ckv", 2), ("ffn0", 8), ("mix1", 8), ("ffn1", 8), ("gmlp", 8), ("dil", 8)):
            SPLITS[name] = c
            c += chunks
        MODS_READ = {"mix0": FIRST_MODS // 2, "ffn0": (FIRST_MODS + 4 * MLA_MODS + OUT_MODS) // 2, "mix1": 48}
        GQA_U, GQA_W, GQA_X, GQA_Q = 10, 8, 4, 70
        DIL_U, DIL_W, DIL_X, DIL_U0, DIL_W0, DIL_X0 = 18, 8, 4, 110, 72, 40
        MLA_U, MLA_W, MLA_X = 16, 10, 6

        def acc_main(u):
            return PS[:, u.nth % 3, :]

        def acc_ctx(u):
            return PS[:, 3 + u.nth % 3, 0:TC]

        def row(u):
            b = u.mod(2) * 1024
            return psf[:, b + TC:b + 1024]

        ST_M, ST_C = PS[:, 6, :], PS[:, 7, 0:TC]

        MOD_ROW, MOD_COL = PS[0:2, 6, 0:2 * P], PS[:, 7, 0:4]

        def out_half(x):
            return PS[:, 6 + x.mod(2), 0:256]

        def pt_views(n, x, pt):
            src = psf[:, 4 * 512:4 * 512 + (4 if n == 0 else 6) * P]
            if n == 0:
                return (pt[:, x.mod(2), 0:2, :].rearrange("p b (q n) -> p q b n", q=2), src.rearrange("p (q b n) -> p q b n", q=2, b=2))
            q = (n - 1) % 2
            return pt[:, x.mod(2), :, q * P:(q + 1) * P], src.rearrange("p (b n) -> p b n", b=6)

        def backwards(t):
            return t.rearrange("p (b n) -> p b n", b=4)[:, :, ::-1]

        def forwards(t):
            return t.rearrange("p (b n) -> p b n", b=4)

        LAT_M = [LAT[:, j, TC:TA] for j in range(6)]
        LAT_C = [LAT[:, j, 0:TC] for j in range(6)]

        @block.sync
        def _(sp):
            for s in (0, 1):
                sp.dma_start(RAW[:, s, :], a["tiles"][s]).then_inc(tile_loaded[s], 16)
            pairs = N_TILES // 2
            with sp.Fori(1, pairs) as i:
                for s in (0, 1):
                    sp.wait_ge(tile_split[s], i * 1)
                    sp.dma_start(RAW[:, s, :], a["tiles"][bass.ds(i * 2 + s, 1)].rearrange("a p n -> (a p) n")
                                 ).then_inc(tile_loaded[s], 16)
            if N_TILES % 2:
                sp.wait_ge(tile_split[0], pairs)
                sp.dma_start(RAW[:, 0, :], a["tiles"][N_TILES - 1]).then_inc(tile_loaded[0], 16)
            for j in range(KC):
                sp.wait_ge(x_ready, 2 * KC + j + 1)
                sp.dma_start(out[:, j, :], X_M[:, j, :]).then_inc(stored, 16)
            sp.wait_ge(stored, 16 * KC)

        @block.gpsimd
        def _(pool):
            for s in (0, 1):
                pool.dma_start(MRAW[:, s, :], a["mods"][s]).then_inc(mod_loaded[s], 16)
            pool.dma_start(ONEHOT[:, :], a["onehot"]).then_inc(rel_loaded, 16)
            pool.dma_start(RELMASK[:, :], a["relmask"]).then_inc(rel_loaded, 16)
            pool.dma_start(REL[:, :], a["rel"]).then_inc(rel_loaded, 16)
            with pool.Fori(1, 48) as i:
                for s in (0, 1):
                    pool.wait_ge(mod_done, i * 2 + s - 1)
                    pool.dma_start(MRAW[:, s, :], a["mods"][bass.ds(i * 2 + s, 1)].rearrange("a p n -> (a p) n")
                                   ).then_inc(mod_loaded[s], 16)
            pool.wait_ge(norm_scaled, SPLITS["ffn1"])
            pool.dma_start(ROPE_TG[:, :, :], a["rope_c"]).then_inc(rope_c_loaded, 16)
            pool.wait_ge(acc_done, UNIT["gmlp_v"])
            for n in range(2):
                pool.dma_start(VN_GB[:, n, :], bass.AP(a["gm_rows"].tensor, n * 2048, [[0, P], [1, 2048]])).then_inc(rows_loaded, 16)
            pool.dma_start(BS[:, :], bass.AP(a["gm_rows"].tensor, 2 * 2048, [[0, P], [1, 2048]])).then_inc(rows_loaded, 16)
            pool.memset(Y[:, :, :], 0.0).then_inc(y_zero, 1)
            pool.wait_ge(bias_stored, 16)
            pool.wait_ge(acc_done, UNIT["dil_out"])

            def bias_tile(row0, h):
                src = bass.AP(dt_scratch.tensor, row0 * (NREL * TW), [[1, P], [TW, NREL], [1, P]])
                pool.dma_start(TB[:, h, :, :], src).then_inc(tb_loaded[h], 16)

            for h in range(2):
                bias_tile(h, h)
            with pool.Fori(1, 8) as i:
                for h in range(2):
                    pool.wait_ge(both_max, At(DIL_W * -1 + 4 * (h + 1), DIL_W, i).times())
                    bias_tile(i * 2 + h, h)

        @block.tensor
        def _(pe):
            def three(out_, wh, wl, xh, xl, first, last):
                pe.matmul(out_, wh, xh, start=first, stop=False, skip_group_check=True)
                pe.matmul(out_, wh, xl, start=False, stop=False, skip_group_check=True)
                return pe.matmul(out_, wl, xh, start=False, stop=last, skip_group_check=True)

            def tile_ready(s):
                pe.wait_ge(tile_split[s.mod(2)], s.over(2).times(1, 1))

            def mod_rows(j, banks_free=None):
                if banks_free is not None:
                    pe.wait_ge(*banks_free)
                if j.i is not None or j.start:
                    pe.wait_ge(mod_read, j.times())
                for s in range(2):
                    pe.wait_ge(mod_loaded[s], j.times(16, 16))
                    for k in range(KC):
                        mm = pe.matmul(MOD_ROW[:, s * P:(s + 1) * P], CVEC[:, k, :], MRAW[:, s, k * P:(k + 1) * P],
                                       start=(k == 0), stop=(k == KC - 1), skip_group_check=True)
                    mm.then_inc(mod_done, 1)

            def mod_turn(j):
                pe.wait_ge(mod_row, j.times(1, 1))
                for s in range(2):
                    mm = pe.matmul(MOD_COL[:, 2 * s:2 * s + 2], MROW[:, s * P:(s + 1) * P], IDENT[0:2, 0:2], start=True, stop=True,
                                   skip_group_check=True)
                mm.then_inc(mod_turned, 1)

            def mod_chunks(j, n, banks_free=None):
                for m in range(n // 2):
                    mod_rows(j.over(2) + m, banks_free if m == 0 else None)
                    mod_turn(j.over(2) + m)

            def stats(name, chunks, ctx_too):
                n, c0 = NORM[name]
                if name in MODS_READ:
                    pe.wait_ge(mod_read, MODS_READ[name])
                for j in range(chunks):
                    pe.wait_ge(sq_ready, c0 + j + 1)
                    if ctx_too:
                        pe.matmul(ST_C, ONES[:, :], SQ[:, (c0 + j) % 2, 0:TC], start=(j == 0), stop=(j == chunks - 1), skip_group_check=True)
                    pe.matmul(ST_M, ONES[:, :], SQ[:, (c0 + j) % 2, TC:TA], start=(j == 0), stop=(j == chunks - 1), skip_group_check=True
                              ).then_inc(sq_used, 1)

            def gemm(s, u, xm, xc=None, off=0, stride=P, kn=KC, ready=None, new_tile=True):
                if new_tile:
                    tile_ready(s)
                if u.nth == 0:
                    pe.wait_ge(acc_read, u.times())
                elif u.nth >= 3:
                    pe.wait_ge(acc_read, (u - 2).times())
                for k in range(kn):
                    if ready is not None:
                        pe.wait_ge(ready[0], ready[1].times(1, k + 1))
                    c = off + k * stride
                    wh, wl = WH[:, s.mod(2), c:c + P], WL[:, s.mod(2), c:c + P]
                    if xc is not None:
                        three(acc_ctx(u), wh, wl, xc[0][:, k, :], xc[1][:, k, :], k == 0, k == kn - 1)
                    mm = three(acc_main(u), wh, wl, xm[0][:, k, :], xm[1][:, k, :], k == 0, k == kn - 1)
                mm.then_inc(acc_done, 1)

            pe.wait_ge(silu_ready, 1)
            pe.wait_ge(params_loaded, 48)
            pe.wait_ge(ones_ready, 4)
            mod_chunks(At(0), FIRST_MODS)
            pe.wait_ge(rel_loaded, 48)
            for g, at, n in ((1, 0, TW), (2, TW, TW), (0, 2 * TW, 2 * TW), (0, 4 * TW, 2 * TW), (0, 6 * TW, 2 * TW), (0, 8 * TW, TW)):
                mm = pe.matmul(psf[0:B_HEADS, at:at + n], REL[:, g * B_HEADS:(g + 1) * B_HEADS], ONEHOT[:, at:at + n], start=True, stop=True)
            mm.then_inc(bias_sum, 1)
            stats("mix0", 8, True)

            s, u = At(TILES["pool_in"]), At(UNIT["in"])
            pe.wait_ge(bias_ready, 1)
            for n in range(10):
                gemm(s + n, u + n, HM, HC, ready=(norm_ready, At(SPLITS["mix0"])) if n == 0 else None)
            s = At(TILES["pool_w"])
            tile_ready(s)
            for g in range(4):
                u = At(UNIT["pool_w"]) + g
                pe.wait_ge(acc_read, u.times() if g == 0 else (u - 2).times())
                pe.wait_ge(pool_ready, g + 1)
                w = slice(g * P, (g + 1) * P)
                three(acc_ctx(u), WH[:, s.mod(2), w], WL[:, s.mod(2), w], GC[0][:, g, :], GC[1][:, g, :], True, True)
                three(acc_main(u), WH[:, s.mod(2), w], WL[:, s.mod(2), w], GM[0][:, g, :], GM[1][:, g, :], True, True
                      ).then_inc(acc_done, 1)
            stats("cq", 3, True)
            stats("ckv", 2, True)
            pe.wait_ge(acc_read, UNIT["mix_out"])

            def slot(u):
                pe.wait_ge(score_free[u.mod(2)], u.over(2).times(1, 1))

            def transposes(w, blocks, rows):
                pe.wait_ge(prob_ready, w.times(1, 1))
                pe.wait_ge(pt_ready, w.times(1, 1))
                for b in range(blocks):
                    mm = pe.transpose(psf[:, 4 * 512 + b * P:4 * 512 + (b + 1) * P], rows[:, b * P:(b + 1) * P], IDENT[:, :])
                mm.then_inc(pt_done, 1)

            def attend(units, scores, values, rows=lambda w: PROB[:, w.mod(2), :]):
                scores(0)
                scores(1)
                last = None
                for n, (w, blocks, half) in enumerate(units):
                    if n + 2 < len(units):
                        scores(n + 2)
                    transposes(w, blocks, rows(w))
                    if last is not None:
                        values(*last)
                    last = (half, w) if half is not None else None
                values(*last)

            def half_starts(x, w):
                pe.wait_ge(pt_ready, w.times(1, 2))
                pe.wait_ge(o_read, x.times(1, 1))
                return out_half(x)

            pe.wait_ge(norm_ready, SPLITS["ffn0"])
            with pe.Fori(0, 4) as i:
                s = At(TILES["mla"], 2, i)
                u = At(0, MLA_U, i)
                tile_ready(s)
                for h in range(2):
                    slot(u + h)
                    for part in (slice(0, TC), slice(TC, TA)):
                        for k in range(3):
                            c = k * 2 * DH_A + h * DH_A
                            mm = three(row(u + h)[0:DH_A, part], WH[:, s.mod(2), c:c + DH_A], WL[:, s.mod(2), c:c + DH_A],
                                       CQ[0][:, k, part], CQ[1][:, k, part], k == 0, k == 2)
                    mm.then_inc(score_done, 1)
                t = s + 1
                tile_ready(t)
                for h in range(2):
                    slot(u + 2 + h)
                    for part in (slice(0, TC), slice(TC, TA)):
                        for k in range(2):
                            c = k * P + h * NOPE
                            mm = three(row(u + 2 + h)[0:NOPE, part], WH[:, t.mod(2), c:c + NOPE], WL[:, t.mod(2), c:c + NOPE],
                                       CKV[0][:, k, part], CKV[1][:, k, part], k == 0, k == 1)
                    mm.then_inc(score_done, 1)
                for v in range(2):
                    uu = u + 4 + v
                    slot(uu)
                    for b in range(3):
                        tok = slice((3 * v + b) * P, (3 * v + b + 1) * P)
                        o = psf[:, uu.mod(2) * 1024 + b * P:uu.mod(2) * 1024 + (b + 1) * P]
                        for k in range(2):
                            c = 2 * P + k * P
                            mm = three(o, CKV[0][:, k, tok], CKV[1][:, k, tok], WH[:, t.mod(2), c:c + P], WL[:, t.mod(2), c:c + P],
                                       k == 0, k == 1)
                    mm.then_inc(score_done, 1)
                mod_chunks(At(FIRST_MODS, MLA_MODS, i), MLA_MODS, (o_read, At(0, MLA_X, i).times(1, 2)))
                pe.wait_ge(mod_read, At((FIRST_MODS + MLA_MODS) // 2, MLA_MODS // 2, i).times())
                uu = u + 5
                pe.wait_ge(score_free[uu.mod(2)], uu.over(2).times(1, 2))
                w0, x0 = At(0, MLA_W, i), At(0, MLA_X, i)
                units = []
                for h in range(2):
                    for n in range(5):
                        half = None if n in (1, 3) else x0 + (3 * h + (n + 1) // 2)
                        units.append((w0 + 5 * h + n, 4 if n == 0 else 6, half))

                def scores(n):
                    uu, h, n = u + 6 + n, n // 5, n % 5
                    slot(uu)
                    if n == 0:
                        for q in range(2):
                            qs = slice(q * P, (q + 1) * P)
                            mm = three(row(uu)[:, q * TC:(q + 1) * TC], QA[0][0:DH_A, h, qs], QA[1][0:DH_A, h, qs],
                                       KA[0][0:DH_A, h, 0:TC], KA[1][0:DH_A, h, 0:TC], True, True)
                    else:
                        qs = slice(TC + (n - 1) * P, TC + n * P)
                        for part in (slice(0, TC), slice(TC, TA)):
                            mm = three(row(uu)[:, part], QA[0][0:DH_A, h, qs], QA[1][0:DH_A, h, qs],
                                       KA[0][0:DH_A, h, part], KA[1][0:DH_A, h, part], True, True)
                    mm.then_inc(score_done, 1)

                def values(x, w):
                    keys = 2 if (x.start - x0.start) % 3 == 0 else 6
                    o = half_starts(x, w)
                    for b in range(keys):
                        mm = three(o, VA[0][:, b, :], VA[1][:, b, :], PTA[0][:, x.mod(2), b, :], PTA[1][:, x.mod(2), b, :],
                                   b == 0, b == keys - 1)
                    mm.then_inc(o_done, 1)

                attend(units, scores, values)
            pe.wait_ge(o_read, 4 * MLA_X + 2)
            mod_chunks(At(FIRST_MODS + 4 * MLA_MODS), OUT_MODS)

            def out_projection(tile, unit, ctx_too):
                with pe.Fori(0, 2) as i:
                    for m in range(4):
                        gemm(At(tile, 4, i) + m, At(unit, 4, i) + m, GM, GC if ctx_too else None)

            out_projection(TILES["mix_out"], UNIT["mix_out"], True)

            def ffn(layer, ctx_too, mods):
                name = f"ffn{layer}"
                stats(name, KC, ctx_too)
                hc, gc = (HC, GC) if ctx_too else (None, None)

                def group(i, n0, count, chunk_waits):
                    s = At(TILES[name] + 3 * n0, 12, i)
                    u = At(UNIT[name] + 4 * n0, 16, i)
                    f = At(layer * FC + n0, 4, i)
                    u0 = u
                    for n in range(count):
                        pair = At((FIRST_MODS + 4 * MLA_MODS + OUT_MODS) // 2 + n0 + n, 4, i)
                        for m in range(2):
                            gemm(s + (2 * n + m), u + (2 * n + m), HM, hc,
                                 ready=(norm_ready, At(SPLITS[name])) if chunk_waits and n + m == 0 else None)
                            if mods:
                                (mod_turn if m else mod_rows)(pair)
                    s, u = s + 2 * count, u + 2 * count
                    per_tile = KC // count
                    for m in range(KC):
                        gemm(s + m // per_tile, u + m, GM, gc, off=(m % per_tile) * P, stride=per_tile * P, kn=count,
                             ready=(gated_ready, f) if m == 0 else None, new_tile=m % per_tile == 0)

                with pe.Fori(0, 5) as i:
                    group(i, 0, 4, True)
                group(None, 20, 2, False)

            ffn(0, True, True)

            stats("mix1", KC, True)
            pe.wait_ge(acc_read, UNIT["gqa_out"])

            def token_chunk(b):
                t, c = (HC, b * P) if b < 2 else (HM, (b - 2) * P)
                return lambda k: (t[0][:, k, c:c + P], t[1][:, k, c:c + P])

            def head_sums(m, n, w, ctx_too):
                pe.wait_ge(head_sq, m.times(1, 1))
                if n == 0:
                    pe.wait_ge(pt_ready, w.times(1, 1))
                elif ctx_too:
                    pe.wait_ge(head_rms, m.times())
                if ctx_too:
                    pe.matmul(PS[:, 5, 0:TC], ONES[:, :], SQ[:, m.mod(2), 0:TC], start=True, stop=True)
                b = 4 if ctx_too else 4 + n
                pe.matmul(PS[:, b, :], ONES[:, :], SQ[:, m.mod(2), TC:TA], start=True, stop=True).then_inc(head_sum, 1)

            s, u = At(TILES["gqa_kv"]), At(4 * MLA_U)
            for n in range(2):
                tile_ready(s + n)
                slot(u + n)
                for k in range(KC):
                    if n == 0:
                        pe.wait_ge(norm_ready, SPLITS["mix1"] + k + 1)
                    c = slice(k * P, (k + 1) * P)
                    wh, wl = WH[:, (s + n).mod(2), c], WL[:, (s + n).mod(2), c]
                    three(row(u + n)[:, 0:TC], wh, wl, HC[0][:, k, :], HC[1][:, k, :], k == 0, k == KC - 1)
                    mm = three(row(u + n)[:, TC:TA], wh, wl, HM[0][:, k, :], HM[1][:, k, :], k == 0, k == KC - 1)
                mm.then_inc(score_done, 1)
            for n in range(2):
                head_sums(At(n), n, At(4 * MLA_W), True)
            for n in range(2):
                tile_ready(s + 2 + n)
                for v in range(2):
                    uu = u + 2 + 2 * n + v
                    slot(uu)
                    for b in range(3):
                        x = token_chunk(3 * v + b)
                        for k in range(KC):
                            c = slice(k * P, (k + 1) * P)
                            o = psf[:, uu.mod(2) * 1024 + b * P:uu.mod(2) * 1024 + (b + 1) * P]
                            mm = three(o, *x(k), WH[:, (s + 2 + n).mod(2), c], WL[:, (s + 2 + n).mod(2), c], k == 0, k == KC - 1)
                    mm.then_inc(score_done, 1)
            for kv in range(2):
                with pe.Fori(0, 2) as i:
                    s, u = At(TILES["gqa_q"] + 4 * kv, 2, i), At(GQA_Q + 2 * GQA_U * kv, GQA_U, i)
                    w0 = At(4 * MLA_W + 2 * GQA_W * kv, GQA_W, i)
                    x0 = At(4 * MLA_X + 2 * GQA_X * kv, GQA_X, i)
                    m = At(2 + 4 * kv, 2, i)
                    for h in range(2):
                        t = s + h
                        tile_ready(t)
                        slot(u + h)
                        for k in range(KC):
                            c = slice(k * P, (k + 1) * P)
                            mm = three(row(u + h)[:, TC:TA], WH[:, t.mod(2), c], WL[:, t.mod(2), c], HM[0][:, k, :], HM[1][:, k, :], k == 0, k == KC - 1)
                            if h and k == 1:
                                head_sums(m, 0, w0, False)
                        mm.then_inc(score_done, 1)
                    head_sums(m + 1, 1, w0, False)

                    def scores(n):
                        uu, h, q = u + 2 + n, n // 4, n % 4
                        if q == 0:
                            pe.wait_ge(head_split, (m + h).times(1, 1))
                        slot(uu)
                        qs = slice(q * P, (q + 1) * P)
                        for part in (slice(0, TC), slice(TC, TA)):
                            mm = three(row(uu)[:, part], QG[0][:, h, qs], QG[1][:, h, qs], KG[0][:, kv, part], KG[1][:, kv, part], True, True)
                        mm.then_inc(score_done, 1)

                    def values(x, w):
                        o = half_starts(x, w)
                        for b in range(6):
                            mm = three(o, VG[0][:, b, kv, :], VG[1][:, b, kv, :], PTG[0][:, x.mod(2), b, :], PTG[1][:, x.mod(2), b, :],
                                       b == 0, b == 5)
                        mm.then_inc(o_done, 1)

                    attend([(w0 + n, 6, None if n % 2 == 0 else x0 + n // 2) for n in range(8)], scores, values)
            pe.wait_ge(o_read, 4 * MLA_X + 4 * GQA_X + 2)
            out_projection(TILES["gqa_out"], UNIT["gqa_out"], False)
            ffn(1, False, False)

            stats("final", KC, False)
            stats("gmlp", KC, False)
            pe.wait_ge(acc_read, UNIT["gmlp_v"])
            with pe.Fori(0, 2) as i:
                for g in range(2):
                    s, u = At(TILES["gmlp_v"] + 4 * g, 8, i), At(UNIT["gmlp_v"] + 4 * g, 8, i)
                    pe.wait_ge(acc_read, (u - 4).times())
                    for t in range(4):
                        tile_ready(s + t)
                        for b in range(4):
                            for k in range(2):
                                kk = 2 * t + k
                                if g == 0 and b == 0:
                                    pe.wait_ge(norm_ready, SPLITS["gmlp"] + kk + 1)
                                tok, c = slice(b * P, (b + 1) * P), slice(k * TM, (k + 1) * TM)
                                mm = three(PS[:, 4 * g + b, :], HM[0][:, kk, tok], HM[1][:, kk, tok],
                                           WH[:, (s + t).mod(2), c], WL[:, (s + t).mod(2), c], kk == 0, kk == KC - 1)
                            if t == 3:
                                mm.then_inc(acc_done, 1)
                        if t < 3:
                            mm.then_inc(v_tile_done, 1)
            with pe.Fori(0, 4) as i:
                s, u, f = At(TILES["gmlp"], 12, i), At(UNIT["gmlp"], 20, i), At(0, 4, i)
                for h in range(4):
                    gemm(s + 2 * h, u + 3 * h, HM)
                    gemm(s + (2 * h + 1), u + (3 * h + 1), HM)
                    uu = u + (3 * h + 2)
                    if uu.nth >= 3:
                        pe.wait_ge(acc_read, (uu - 2).times())
                    pe.wait_ge(vs_ready, (f + h).times(1, 2))
                    for b in range(4):
                        ws = [w[:, bass.ds((f + h).times(P), P)] for w in WS]
                        mm = three(acc_main(uu)[:, b * P:(b + 1) * P], VS[0][:, b, :], VS[1][:, b, :], ws[0], ws[1], True, True)
                    mm.then_inc(acc_done, 1)
                for m in range(KC):
                    gemm(s + (8 + m // 2), u + (12 + m), PG, off=(m % 2) * P, stride=2 * P, kn=4,
                         ready=(gm_ready, f + 1) if m == 0 else None, new_tile=m % 2 == 0)
            stats("gmlp_post", KC, False)

            stats("dil", KC, False)
            pe.wait_ge(acc_read, UNIT["dil_out"])
            with pe.Fori(0, 8) as i:
                s, u = At(TILES["dil"], 10, i), At(DIL_U0, DIL_U, i)
                w0, x0 = At(DIL_W0, DIL_W, i), At(DIL_X0, DIL_X, i)
                for n in range(10):
                    t, uu = s + n, u + n
                    tile_ready(t)
                    slot(uu)
                    for k in range(KC):
                        if n == 0:
                            pe.wait_ge(norm_ready, SPLITS["dil"] + k + 1)
                        c = slice(k * P, (k + 1) * P)
                        mm = three(row(uu)[:, TC:TA], WH[:, t.mod(2), c], WL[:, t.mod(2), c], HM[0][:, k, :], HM[1][:, k, :], k == 0, k == KC - 1)
                    mm.then_inc(score_done, 1)
                    if n in (4, 5):
                        pe.wait_ge(pt_ready, w0.times(1, 1))
                        for g in (0, 1) if n == 4 else (2,):
                            v = u + g
                            pe.wait_ge(score_free[v.mod(2)], v.over(2).times(1, 2))
                            if g == 2:
                                pe.wait_ge(vt_read, At(0, 3, i).times(1, 1))
                            for b in range(4):
                                mm = pe.transpose(PS[:, 4 + g % 2, b * P:(b + 1) * P], VF[:, g, b * P:(b + 1) * P], IDENT[:, :])
                            mm.then_inc(vt_done, 1)
                last = u + 9
                pe.wait_ge(score_free[last.mod(2)], last.over(2).times(1, 2))
                pe.wait_ge(vt_read, At(0, 3, i).times(1, 3))

                def scores(n):
                    uu, h, r = u + 10 + n, n // 4, n % 4
                    slot(uu)
                    rows, blk = slice(h * 64, h * 64 + 64), slice(r * P, (r + 1) * P)
                    for g, dst, keys in ((1, slice(0, P), blk), (2, slice(P, 2 * P), blk), (0, slice(TC, TA), slice(0, TM))):
                        mm = three(row(uu)[:, dst], QD[0][rows, g, blk], QD[1][rows, g, blk], KD[0][rows, g, keys], KD[1][rows, g, keys],
                                   True, True)
                    mm.then_inc(score_done, 1)

                def values(x, w):
                    o, half = half_starts(x, w), (x.start - x0.start) % 2
                    for b in range(4):
                        three(o, VD[0][:, 0, b, :], VD[1][:, 0, b, :], PTD[0][:, x.mod(2), 2 + b, :], PTD[1][:, x.mod(2), 2 + b, :],
                              b == 0, False)
                    for g in (1, 2):
                        for q in range(2):
                            qs, r = slice(q * P, (q + 1) * P), 2 * half + q
                            mm = three(o[:, qs], VD[0][:, g, r, :], VD[1][:, g, r, :], PTD[0][:, x.mod(2), g - 1, qs],
                                       PTD[1][:, x.mod(2), g - 1, qs], False, g == 2)
                    mm.then_inc(o_done, 1)

                attend([(w0 + n, 6, None if n % 2 == 0 else x0 + n // 2) for n in range(8)], scores, values,
                       lambda w: PROB4[:, w.mod(4), :])
            pe.wait_ge(o_read, DIL_X0 + 8 * DIL_X + 2)
            for m in range(KC):
                gemm(At(TILES["dil_out"] + m), At(UNIT["dil_out"]) + m, DG)
            stats("dil_post", KC, False)
        @block.scalar
        def _(act):
            act.dma_start(CVEC[:, :, :], a["cvec"]).then_inc(params_loaded, 16)
            act.dma_start(COLS[:, :], a["cols"]).then_inc(params_loaded, 16)
            act.dma_start(IDENT[:, :], a["ident"]).then_inc(params_loaded, 16)
            act.dma_start(X_M[:, :, :], a["x"]).then_inc(x_loaded, 16)
            act.dma_start(X_C[:, :, :], a["ctx"]).then_inc(x_loaded, 16)
            act.dma_start(EDGE[:, :, :, :], a["edge"]).then_inc(edge_loaded, 16)

            def copy(out_, in_, scale=1.0):
                return act.activation(out_, in_, ACT.Copy, scale=scale)

            def split(s, after=None):
                if after is not None:
                    act.wait_ge(*after)
                act.wait_ge(tile_loaded[s.mod(2)], s.over(2).times(16, 16))
                copy(WH[:, s.mod(2), :], RAW[:, s.mod(2), :]).then_inc(tile_hi, 1)

            def squares(name, src_m, src_c, ready):
                n, c0 = NORM[name]
                for j in range(len(src_m)):
                    if c0 + j >= 2:
                        act.wait_ge(sq_used, c0 + j - 1)
                    act.wait_ge(*ready(j))
                    if src_c is not None:
                        act.activation(SQ[:, (c0 + j) % 2, 0:TC], src_c[j], ACT.Square)
                    act.activation(SQ[:, (c0 + j) % 2, TC:TA], src_m[j], ACT.Square).then_inc(sq_ready, 1)

            def root(name, chunks, ctx_too, features, scale=1.0, eps=0):
                n, c0 = NORM[name]
                act.wait_ge(sq_used, c0 + chunks)
                if SPLITS.get(name, 0):
                    act.wait_ge(norm_scaled, SPLITS[name])
                k = 1.0 / (features * scale * scale)
                if ctx_too:
                    act.activation(RB[:, 0:TC], ST_C, ACT.Sqrt, bias=CONST[:, eps:eps + 1], scale=k)
                act.activation(RB[:, TC:TA], ST_M, ACT.Sqrt, bias=CONST[:, eps:eps + 1], scale=k).then_inc(rms_ready, 1)

            def shifted(name, dst_m, dst_c, shift):
                c0 = SPLITS[name]
                for j in range(len(dst_m)):
                    act.wait_ge(norm_scaled, c0 + j + 1)
                    t = T[:, (c0 + j) % 2, :]
                    if dst_c is not None:
                        if shift is None:
                            copy(dst_c[j], t[:, 0:TC])
                        else:
                            act.activation(dst_c[j], t[:, 0:TC], ACT.Identity, bias=shift(j, 1))
                    if shift is None:
                        copy(dst_m[j], t[:, TC:TA]).then_inc(norm_hi, 1)
                    else:
                        act.activation(dst_m[j], t[:, TC:TA], ACT.Identity, bias=shift(j, 0)).then_inc(norm_hi, 1)

            def mod_shift(layer, part):
                return lambda j, v: MOD[:, layer * 48 + part * 8 + j, v:v + 1]

            def chunks(t, n=KC):
                return [t[:, j, :] for j in range(n)]

            X_CHUNKS, C_CHUNKS = chunks(X_M), chunks(X_C)

            act.wait_ge(params_loaded, 48)
            act.wait_ge(ones_ready, 4)
            act.activation(CVEC[:, :, :], CVEC[:, :, :], ACT.Silu).then_inc(silu_ready, 1)
            split(At(0))
            split(At(1))
            squares("mix0", X_CHUNKS, C_CHUNKS, lambda j: (x_loaded, 32))
            act.wait_ge(bias_ready, 1)
            act.dma_start(dt_scratch, BVEC[:, :]).then_inc(bias_stored, 16)
            root("mix0", KC, True, D)
            shifted("mix0", chunks(HM[0]), chunks(HC[0]), mod_shift(0, 0))

            for n in range(10):
                split(At(n + 2), (acc_done, UNIT["in"] + n + 1))
                if 1 <= n <= 4:
                    g = n - 1
                    act.wait_ge(pool_diff, g + 1)
                    copy(GC[0][:, g, :], PB[0][:, PAD:PAD + TC])
                    copy(GM[0][:, g, :], PB[0][:, 3 * PAD + TC:3 * PAD + TA]).then_inc(pool_hi, 1)
            for g in range(4):
                u = At(UNIT["pool_w"]) + g
                act.wait_ge(acc_done, u.times(1, 1))
                if g == 3:
                    split(At(TILES["mla"] + 1))
                c = COL["s_pool"] + g
                act.activation(GC[0][:, 4 + g, :], acc_ctx(u), ACT.Copy, scale=COLS[:, c:c + 1])
                act.activation(GM[0][:, 4 + g, :], acc_main(u), ACT.Copy, scale=COLS[:, c:c + 1]).then_inc(poolout_hi, 1)
            squares("cq", LAT_M[0:3], LAT_C[0:3], lambda j: (acc_read, UNIT["in"] + 5 + j))
            root("cq", 3, True, Q_RANK, DH_A ** -0.5, 1)
            squares("ckv", LAT_M[3:5], LAT_C[3:5], lambda j: (acc_read, UNIT["in"] + 8 + j))
            shifted("cq", [CQ[0][:, j, TC:TA] for j in range(3)], [CQ[0][:, j, 0:TC] for j in range(3)], None)
            act.wait_ge(sq_used, NORM["ckv"][1] + 2)
            act.dma_start(ROPE_TA[:, :, :], a["rope_a"]).then_inc(rope_loaded, 16)
            root("ckv", 2, True, KV_RANK)
            shifted("ckv", [CKV[0][:, j, TC:TA] for j in range(2)], [CKV[0][:, j, 0:TC] for j in range(2)], None)
            act.wait_ge(rope_done, 1)
            for h in range(2):
                mm = copy(KA[0][NOPE:DH_A, h, :], LAT[NOPE:DH_A, 5, :])
            mm.then_inc(kr_hi, 1)

            def exps(u, w, rows):
                act.wait_ge(max_ready, w.times(1, 1))
                st = STAT[:, w.mod(2), :]
                at = 0
                for n, width in enumerate(rows):
                    mm = act.activation(PROB[:, w.mod(2), at:at + width], row(u)[:, at:at + width], ACT.Exp,
                                        bias=st[:, n:n + 1], accum_out=st[:, 2 + n:3 + n])
                    at += width
                mm.then_inc(score_free[u.mod(2)], 1)

            def attend(units, exp, high, out_high, meanwhile=None):
                exp(0)
                exp(1)
                if meanwhile:
                    meanwhile()
                before = last = None
                for n, (w, blocks, half) in enumerate(units):
                    act.wait_ge(pt_done, w.times(1, 1))
                    high(n)
                    if n + 2 < len(units):
                        exp(n + 2)
                    if before is not None:
                        out_high(before)
                    before, last = last, half
                for x in (before, last):
                    if x is not None:
                        out_high(x)

            def pt_high(n, x, w, pt):
                b, src = pt_views(n, x, pt)
                return copy(b, src)

            act.wait_ge(bias_stored, 16)
            with act.Fori(0, 4) as i:
                s, u = At(TILES["mla"], 2, i), At(0, MLA_U, i)
                for h in range(2):
                    q = u + h
                    act.wait_ge(score_done, q.times(1, 1))
                    copy(QA[0][0:DH_A, h, 0:TC], row(q)[0:DH_A, 0:TC])
                    act.wait_ge(rope_done, At(h, 2, i).times(1, 2))
                    copy(QA[0][0:DH_A, h, TC:TA], RT[0][0:DH_A, :]).then_inc(proj_hi, 1)
                split(s + 2)
                for h in range(2):
                    act.wait_ge(score_done, (u + 2 + h).times(1, 1))
                    copy(KA[0][0:NOPE, h, :], row(u + 2 + h)[0:NOPE, :]).then_inc(proj_hi, 1)
                for v in range(2):
                    uu = u + 4 + v
                    act.wait_ge(score_done, uu.times(1, 1))
                    copy(VA[0][:, 3 * v:3 * v + 3, :], psf[:, uu.mod(2) * 1024:uu.mod(2) * 1024 + 3 * P].rearrange("p (b n) -> p b n", b=3)
                         ).then_inc(proj_hi, 1)
                split(s + 3)
                w0, x0 = At(0, MLA_W, i), At(0, MLA_X, i)
                units = [(w0 + (5 * h + n), 4 if n == 0 else 6, None if n in (1, 3) else x0 + (3 * h + (n + 1) // 2))
                         for h in range(2) for n in range(5)]

                def exp(n):
                    exps(u + (6 + n), w0 + n, (TC, TC) if n % 5 == 0 else (TA,))

                def high(n):
                    x = x0 + (3 * (n // 5) + (n % 5 + 1) // 2)
                    act.wait_ge(o_done, x.times(1, 1))
                    pt_high(n % 5, x, w0 + n, PTA[0]).then_inc(pt_hi, 1)

                def out_high(x):
                    h, half = (x.start - x0.start) // 3, (x.start - x0.start) % 3
                    act.wait_ge(o_done, x.times(1, 3))
                    rows = slice(h * 64, h * 64 + 64)
                    dst = GC[0][rows, bass.ds(i, 1), :] if half == 0 else GM[0][rows, bass.ds(i, 1), (half - 1) * 256:half * 256]
                    copy(dst.rearrange("p a n -> p (a n)"), out_half(x)[rows]).then_inc(o_hi, 1)

                attend(units, exp, high, out_high)

            def out_projection(tile, unit):
                with act.Fori(0, 2) as i:
                    for m in range(4):
                        split(At(tile + m + 2, 4, i), (acc_done, At(unit + m + 1, 4, i).times()))

            out_projection(TILES["mix_out"], UNIT["mix_out"])

            def ffn(layer, ctx_too):
                name = f"ffn{layer}"
                last = UNIT["mix_out" if layer == 0 else "gqa_out"]
                squares(name, X_CHUNKS, C_CHUNKS if ctx_too else None, lambda j: (acc_read, last + j + 1))
                root(name, KC, ctx_too, D)
                shifted(name, chunks(HM[0]), chunks(HC[0]) if ctx_too else None, mod_shift(layer, 3))
                lo = 0 if ctx_too else TC
                cols = COL[f"conv{layer}"]

                def group(i, n0, count, ahead=True):
                    s, u = At(TILES[name] + 3 * n0, 12, i), At(UNIT[name] + 4 * n0, 16, i)
                    f, fg = At(n0, 4, i), At(layer * FC + n0, 4, i)
                    for n in range(count):
                        sg, ug = s + 2 * n, u + 2 * n
                        split(sg + 2, (acc_done, ug.times(1, 1)))
                        r = (fg + n).mod(2)
                        tap, bias = COLS[:, (f + n).ds(1, 1, cols + FC)], COLS[:, (f + n).ds(1, 1, cols + 3 * FC)]
                        if ctx_too:
                            act.activation(CONV[:, r, 0:TC], acc_ctx(ug), ACT.Identity, scale=tap, bias=bias)
                        act.activation(CONV[:, r, TC:TA], acc_main(ug), ACT.Identity, scale=tap, bias=bias).then_inc(conv_center, 1)
                        act.wait_ge(acc_read, ug.times(1, 1))
                        act.activation(CONV[:, r, lo:TA], CONV[:, r, lo:TA], ACT.Silu).then_inc(silu_done, 1)
                        split(sg + 3, (acc_done, ug.times(1, 2)))
                        act.wait_ge(acc_read, ug.times(1, 2))
                        if ctx_too:
                            copy(GC[0][:, n, :], GATED[:, r, 0:TC])
                        copy(GM[0][:, n, :], GATED[:, r, TC:TA]).then_inc(gated_hi, 1)
                    s, u = s + 2 * count, u + 2 * count
                    per_tile = KC // count
                    if ahead:
                        for t in range(count):
                            split(s + t + 2, (acc_done, (u + per_tile * (t + 1)).times()))

                with act.Fori(0, 5) as i:
                    group(i, 0, 4)
                group(None, 20, 2, layer == 0)

            ffn(0, True)

            def head_root(m, n, ctx_too, eps):
                sq = SQ[:, m.mod(2), :]
                act.wait_ge(head_sum, m.times(1, 1))
                k = 1.0 if eps else 1.0 / P
                if ctx_too:
                    act.activation(sq[:, 0:TC], PS[:, 5, 0:TC], ACT.Sqrt, bias=CONST[:, eps:eps + 1], scale=k)
                act.activation(sq[:, TC:TA], PS[:, 4 if ctx_too else 4 + n, :], ACT.Sqrt, bias=CONST[:, eps:eps + 1], scale=k).then_inc(head_rms, 1)

            squares("mix1", X_CHUNKS, C_CHUNKS, lambda j: (acc_read, UNIT["gqa_out"] - KC + j + 1))
            root("mix1", KC, True, D)
            shifted("mix1", chunks(HM[0]), chunks(HC[0]), mod_shift(1, 0))
            s, u = At(TILES["gqa_kv"]), At(4 * MLA_U)
            for n in range(2):
                split(s + 2 + n, (score_done, (u + n).times(1, 1)))
                act.activation(SQ[:, n, :], row(u + n), ACT.Square).then_inc(head_sq, 1)
            for n in range(2):
                head_root(At(n), n, True, 0)
            for n in range(2):
                act.wait_ge(rope_done, 10 + n)
                copy(KG[0][:, n, 0:TC], HEADN[:, n, 0:TC])
                copy(KG[0][:, n, TC:TA], RG[0][:, :]).then_inc(proj_hi, 1)
            for v in range(4):
                uu = u + 2 + v
                act.wait_ge(score_done, uu.times(1, 1))
                b = 3 * (v % 2)
                copy(VG[0][:, b:b + 3, v // 2, :], psf[:, uu.mod(2) * 1024:uu.mod(2) * 1024 + 3 * P].rearrange("p (b n) -> p b n", b=3)
                     ).then_inc(proj_hi, 1)
                if v % 2:
                    split(s + 4 + v // 2)
            for kv in range(2):
                with act.Fori(0, 2) as i:
                    s, u = At(TILES["gqa_q"] + 4 * kv, 2, i), At(GQA_Q + 2 * GQA_U * kv, GQA_U, i)
                    w0 = At(4 * MLA_W + 2 * GQA_W * kv, GQA_W, i)
                    x0 = At(4 * MLA_X + 2 * GQA_X * kv, GQA_X, i)
                    m = At(2 + 4 * kv, 2, i)
                    def query_high(h):
                        act.wait_ge(rope_done, (m + h).times(1, 10))
                        copy(QG[0][:, h, :], RG[0][:, :]).then_inc(proj_hi, 1)

                    for h in range(2):
                        act.wait_ge(score_done, (u + h).times(1, 1))
                        act.activation(SQ[:, h, TC:TA], row(u + h)[:, TC:TA], ACT.Square).then_inc(head_sq, 1)
                        head_root(m + h, h, False, 2)
                        if h == 0:
                            query_high(0)
                    split(s + 2)
                    split(s + 3)

                    def high(n):
                        x = x0 + n // 2
                        act.wait_ge(o_done, x.times(1, 1))
                        pt_high(n % 4 + 1, x, w0 + n, PTG[0]).then_inc(pt_hi, 1)

                    def out_high(x):
                        act.wait_ge(o_done, x.times(1, 3))
                        h, half = (x.start - x0.start) // 2, (x.start - x0.start) % 2
                        dst = GM[0][:, At(4 * kv + h, 2, i).ds(), half * 256:half * 256 + 256]
                        copy(dst.rearrange("p a n -> p (a n)"), out_half(x)).then_inc(o_hi, 1)

                    attend([(w0 + n, 6, None if n % 2 == 0 else x0 + n // 2) for n in range(8)],
                           lambda n: exps(u + (2 + n), w0 + n, (TA,)), high, out_high, lambda: query_high(1))
            out_projection(TILES["gqa_out"], UNIT["gqa_out"])
            ffn(1, False)

            squares("final", X_CHUNKS, None, lambda j: (acc_read, UNIT["gmlp_v"] - KC + j + 1))
            for n in range(2):
                t = At(TILES["ws"] + n)
                act.wait_ge(tile_loaded[t.mod(2)], t.over(2).times(16, 16))
                copy(WS[0][:, n * D:(n + 1) * D], RAW[:, t.mod(2), :]).then_inc(tile_hi, 1)
            root("final", KC, False, D)
            s = At(TILES["gmlp_v"])
            split(s)
            split(s + 1)
            squares("gmlp", X_CHUNKS, None, lambda j: (x_ready, j + 1))
            root("gmlp", KC, False, D)
            shifted("gmlp", chunks(HM[0]), None, None)
            with act.Fori(0, 2) as i:
                for g in range(2):
                    s, u = At(TILES["gmlp_v"] + 4 * g, 8, i), At(UNIT["gmlp_v"] + 4 * g, 8, i)
                    for t in range(3):
                        split(s + t + 2, (v_tile_done, At(3 * g + t, 6, i).times(1, 1)))
                    split(s + 5, (acc_done, u.times(1, 4)))
                    for b in range(4):
                        act.activation(V[:, b, bass.ds(At(TM * g, 2 * TM, i).times(), TM)], PS[:, 4 * g + b, :], ACT.Gelu_apprx_tanh,
                                       accum_out=LN[:, 0, bass.ds(At(4 * g + b, 8, i).times(), 1)]).then_inc(acc_read, 1)
            act.wait_ge(mean_ready, 2)
            for b in range(4):
                if b:
                    act.wait_ge(var_ready, b)
                act.activation(SQV[:, :], V[:, b, :], ACT.Square, bias=LN[:, 1, b:b + 1], accum_out=LN[:, 2, b:b + 1]).then_inc(var_ready, 1)
            act.wait_ge(var_ready, 4)
            act.activation(LN[:, 3, 0:4], LN[:, 2, 0:4], ACT.Sqrt, bias=CONST[:, 0:1], scale=1.0 / (A_HEADS * P)).then_inc(std_ready, 1)
            with act.Fori(0, 4) as i:
                s, u, f = At(TILES["gmlp"], 12, i), At(UNIT["gmlp"], 20, i), At(0, 4, i)
                for h in range(4):
                    t, uu, fh = s + 2 * h, u + 3 * h, f + h
                    split(t + 2, (acc_done, uu.times(1, 1)))
                    act.wait_ge(v_step, fh.times(2, 2))
                    copy(VS[0][:, :, :], VT[:, :, :]).then_inc(vs_hi, 1)
                    act.wait_ge(acc_read, uu.times())
                    act.activation(UG[:, :], acc_main(uu), ACT.Gelu_apprx_tanh).then_inc(acc_read, 1)
                    split(t + 3, (acc_done, uu.times(1, 2)))
                    act.activation(TH[:, :], acc_main(uu + 1), ACT.Tanh, scale=0.5).then_inc(th_ready, 1)
                    act.wait_ge(y_ready, fh.times(1, 2))
                    copy(PG[0][:, h, :], YG[:, :]).then_inc(gm_hi, 1)
                for m in range(4):
                    split(s + (10 + m), (acc_done, u.times(1, 12 + 2 * m + 2)))
            squares("gmlp_post", chunks(Y), None, lambda j: (acc_read, UNIT["dil_out"] - KC + j + 1))
            root("gmlp_post", KC, False, D)

            squares("dil", X_CHUNKS, None, lambda j: (x_ready, KC + j + 1))
            root("dil", KC, False, D)
            shifted("dil", chunks(HM[0]), None, None)
            with act.Fori(0, 8) as i:
                s, u = At(TILES["dil"], 10, i), At(DIL_U0, DIL_U, i)
                w0, x0 = At(DIL_W0, DIL_W, i), At(DIL_X0, DIL_X, i)
                for n in range(10):
                    t, uu = s + n, u + n
                    act.wait_ge(score_done, uu.times(1, 1))
                    src = row(uu)[:, TC:TA]
                    if n < 3:
                        copy(forwards(VF[:, n, :]), backwards(src)).then_inc(score_free[uu.mod(2)], 1)
                    elif n == 3:
                        act.activation(THG[:, :], src, ACT.Tanh, scale=0.5).then_inc(thg_ready, 1)
                    else:
                        g, is_k = (n - 4) // 2, n % 2
                        if is_k:
                            copy(forwards(KD[0][:, g, :]), backwards(src)).then_inc(dil_hi, 1)
                        else:
                            copy(QD[0][:, g, :], src, 0.125).then_inc(dil_hi, 1)
                    split(t + 2)
                    if n in (4, 5):
                        for g in (0, 1) if n == 4 else (2,):
                            act.wait_ge(vt_done, At(g, 3, i).times(1, 1))
                            copy(VD[0][:, g, :, :].rearrange("p b n -> p (b n)"), PS[:, 4 + g % 2, :]).then_inc(dil_hi, 1)

                def exp(n):
                    w = w0 + n
                    act.wait_ge(both_max, At(n, DIL_W, i).times(1, 1))
                    st = STAT[:, w.mod(2), :]
                    act.activation(PROB4[:, w.mod(4), :], PROB4[:, w.mod(4), :], ACT.Exp, bias=st[:, 0:1], accum_out=st[:, 2:3]
                                   ).then_inc(exp_ready, 1)

                def high(n):
                    x = x0 + n // 2
                    act.wait_ge(o_done, x.times(1, 1))
                    pt_high(n % 4 + 1, x, w0 + n, PTD[0]).then_inc(pt_hi, 1)

                def out_high(x):
                    h, half = (x.start - x0.start) // 2, (x.start - x0.start) % 2
                    rows = slice(h * 64, h * 64 + 64)
                    act.wait_ge(o_scaled, At(x.start - DIL_X0, DIL_X, i).times(1, 1))
                    dst = DG[0][rows, bass.ds(i, 1), half * 256:half * 256 + 256]
                    copy(dst.rearrange("p a n -> p (a n)"), OG[rows, :]).then_inc(o_hi, 1)

                attend([(w0 + n, 6, None if n % 2 == 0 else x0 + n // 2) for n in range(8)], exp, high, out_high)
            for m in range(KC - 2):
                split(At(TILES["dil_out"] + m + 2), (acc_done, UNIT["dil_out"] + m + 1))
            squares("dil_post", chunks(YD), None, lambda j: (acc_read, UNIT["dil_out"] + j + 1))
            root("dil_post", KC, False, D)
        @block.vector
        def _(dve):
            def split(s):
                dve.wait_ge(tile_hi, s.times(1, 1))
                dve.tensor_tensor(WL[:, s.mod(2), :], RAW[:, s.mod(2), :], f32(WH[:, s.mod(2), :]), ALU.subtract
                                  ).then_inc(tile_split[s.mod(2)], 1)

            def f32(ap):
                return ap.bitcast(F32)

            def low(dst, src, high):
                return dve.tensor_tensor(dst, src, f32(high), ALU.subtract)

            def mod_take(j):
                dve.wait_ge(mod_done, j.times(2, 2))
                dve.tensor_copy(MROW[:, :], MOD_ROW).then_inc(mod_row, 1)

            def mod_add(j):
                dve.wait_ge(mod_turned, j.times(1, 1))
                dve.tensor_tensor(MOD[:, j.ds(2, 2), :], MOD_COL.rearrange("p (a v) -> p a v", a=2),
                                  COLS[:, j.ds(2, 2, COL["b_mod"])].unsqueeze(2).to_broadcast([P, 2, 2]), ALU.add).then_inc(mod_read, 1)

            def mods(j, n):
                for m in range(n // 2):
                    mod_take(j.over(2) + m)
                    mod_add(j.over(2) + m)

            def scale1(n, layer, part):
                dve.wait_ge(mod_read, (layer * 48 + part * 8 + 8) // 2)
                dve.tensor_scalar(SCALE1[:, :, :], MOD[:, layer * 48 + part * 8:layer * 48 + part * 8 + 8, :], 1.0, None, ALU.add
                                  ).then_inc(scale1_ready, 1)
                dve.wait_ge(scale1_ready, n + 1)

            def inverse(name, lo=0):
                n, c0 = NORM[name]
                dve.wait_ge(rms_ready, n + 1)
                dve.reciprocal(RB[:, lo:TA], RB[:, lo:TA]).then_inc(rb_ready, 1)
                dve.wait_ge(rb_ready, n + 1)

            def scaled(name, src_m, src_c, dst_m, dst_c, gain, shift, reorder=False):
                c0 = SPLITS[name]

                def low_part(j):
                    t = T[:, (c0 + j) % 2, :]
                    dve.wait_ge(norm_hi, c0 + j + 1)
                    if dst_c is not None:
                        if shift is None:
                            low(dst_c[1][j], t[:, 0:TC], dst_c[0][j])
                        else:
                            dve.scalar_tensor_tensor(out=dst_c[1][j], in0=t[:, 0:TC], scalar=shift(j, 1), in1=f32(dst_c[0][j]),
                                                     op0=ALU.add, op1=ALU.subtract)
                    if shift is None:
                        low(dst_m[1][j], t[:, TC:TA], dst_m[0][j]).then_inc(norm_ready, 1)
                    else:
                        dve.scalar_tensor_tensor(out=dst_m[1][j], in0=t[:, TC:TA], scalar=shift(j, 0), in1=f32(dst_m[0][j]),
                                                 op0=ALU.add, op1=ALU.subtract).then_inc(norm_ready, 1)

                for j in range(len(src_m)):
                    t = T[:, (c0 + j) % 2, :]
                    if c0 + j >= 2:
                        dve.wait_ge(norm_ready, c0 + j - 1)
                    if src_c is not None:
                        dve.scalar_tensor_tensor(out=t[:, 0:TC], in0=src_c[j], scalar=gain(j, 1), in1=RB[:, 0:TC], op0=ALU.mult, op1=ALU.mult)
                    tt, x, rb = t[:, TC:TA], src_m[j], RB[:, TC:TA]
                    if reorder:
                        tt, x, rb = tt.rearrange("p (r l) -> p r l", r=4), by_residue(x), by_residue(rb)
                    dve.scalar_tensor_tensor(out=tt, in0=x, scalar=gain(j, 0), in1=rb, op0=ALU.mult, op1=ALU.mult).then_inc(norm_scaled, 1)
                    if j >= 1:
                        low_part(j - 1)
                low_part(len(src_m) - 1)

            def mod_shift(layer, part):
                return lambda j, v: MOD[:, layer * 48 + part * 8 + j, v:v + 1]

            def scale1_gain(j, v):
                return SCALE1[:, j, v:v + 1]

            def gain_cols(name):
                return lambda j, v: COLS[:, COL[name] + j:COL[name] + j + 1]

            def chunks(t, n=KC):
                return [t[:, j, :] for j in range(n)]

            def both(ts, n=KC):
                return [chunks(ts[0], n), chunks(ts[1], n)]

            X_CHUNKS, C_CHUNKS = chunks(X_M), chunks(X_C)

            dve.memset(ONES[:, :], 1.0).then_inc(ones_ready, 1)
            dve.memset(CONST[:, 0:1], EPS).then_inc(ones_ready, 1)
            dve.memset(CONST[:, 1:2], EPS * DH_A).then_inc(ones_ready, 1)
            dve.memset(CONST[:, 2:3], EPS * P).then_inc(ones_ready, 1)
            for b in PB:
                mm = dve.memset(b[:, :], 0.0)
            mm.then_inc(pad_zero, 1)
            for n, q in enumerate((score_free[0], score_free[1], pt_ready, o_done, o_done, o_read, o_read, vs_ready, y_ready, gm_ready)):
                dve.memset(CONST[:, 8 + n:9 + n], 0.0).then_inc(q, 1)
            split(At(0))
            split(At(1))
            dve.wait_ge(params_loaded, 48)
            mods(At(0), FIRST_MODS)
            dve.wait_ge(bias_sum, 1)
            dve.tensor_tensor(BVEC[:, :], psf[0:B_HEADS, 0:NREL * TW], RELMASK[:, :], ALU.add).then_inc(bias_ready, 1)
            scale1(0, 0, 1)
            inverse("mix0")
            scaled("mix0", X_CHUNKS, C_CHUNKS, both(HM), both(HC), scale1_gain, mod_shift(0, 0))

            body = slice(PAD, PLEN - PAD)
            c_seg, m_seg = slice(PAD, PAD + TC), slice(3 * PAD + TC, 3 * PAD + TA)

            def pool_group(g, n_steps):
                def step(ins):
                    n_steps[0] += 1
                    ins.then_inc(pool_step, 1)
                    dve.wait_ge(pool_step, n_steps[0])

                src = 0
                for level in range(g + 1):
                    dst = 1 if src in (0, 2) else 2
                    m = 1 if level == 0 else 1 << (level - 1)
                    if level == 0:
                        step(dve.tensor_tensor(PB[dst][:, 1:PLEN], PB[src][:, 1:PLEN], PB[src][:, 0:PLEN - 1], ALU.add))
                    else:
                        e = (1 << level) - 1
                        step(dve.tensor_tensor(PB[dst][:, e:PLEN - e], PB[src][:, e + m:PLEN - e + m], PB[src][:, e - m:PLEN - e - m], ALU.add))
                    src = dst
                for seg, (a0, a1) in enumerate(((PAD, PAD + TC), (3 * PAD + TC, 3 * PAD + TA))):
                    for e, at in enumerate((a0, a1 - PAD)):
                        ins = dve.tensor_tensor(PB[src][:, at:at + PAD], PB[src][:, at:at + PAD], EDGE[:, g, 2 * seg + e, :], ALU.mult)
                step(ins)
                dve.scalar_tensor_tensor(out=PB[0][:, body], in0=PB[src][:, body], scalar=1.0 / WINDOWS[g], in1=PB[0][:, body],
                                         op0=ALU.mult, op1=ALU.subtract).then_inc(pool_diff, 1)
                dve.wait_ge(pool_diff, g + 1)

            dve.wait_ge(edge_loaded, 16)
            dve.wait_ge(pad_zero, 1)
            n_steps = [0]
            for n in range(10):
                u = At(UNIT["in"]) + n
                if 1 <= n <= 4:
                    g = n - 1
                    dve.wait_ge(pool_hi, g + 1)
                    low(GC[1][:, g, :], PB[0][:, c_seg], GC[0][:, g, :])
                    low(GM[1][:, g, :], PB[0][:, m_seg], GM[0][:, g, :]).then_inc(pool_ready, 1)
                split(At(n + 2))
                dve.wait_ge(acc_done, u.times(1, 1))
                if n < 4:
                    if n > 0:
                        for at in (PAD + TC,):
                            n_steps[0] += 1
                            dve.memset(PB[0][:, at:at + 2 * PAD], 0.0).then_inc(pool_step, 1)
                            dve.wait_ge(pool_step, n_steps[0])
                    dve.tensor_copy(PB[0][:, c_seg], acc_ctx(u))
                    dve.tensor_copy(PB[0][:, m_seg], acc_main(u)).then_inc(acc_read, 1)
                    dve.wait_ge(acc_read, u.times(1, 1))
                    pool_group(n, n_steps)
                else:
                    r = slice(NOPE, DH_A) if n == 9 else slice(0, P)
                    dve.tensor_copy(LAT_C[n - 4][r], acc_ctx(u)[r])
                    dve.tensor_copy(LAT_M[n - 4][r], acc_main(u)[r]).then_inc(acc_read, 1)
            for g in range(4):
                u = At(UNIT["pool_w"]) + g
                if g == 3:
                    split(At(TILES["mla"] + 1))
                dve.wait_ge(poolout_hi, g + 1)
                c = COL["s_pool"] + g
                for hi, lo, src in ((GC[0], GC[1], acc_ctx(u)), (GM[0], GM[1], acc_main(u))):
                    ins = dve.scalar_tensor_tensor(out=lo[:, 4 + g, :], in0=src, scalar=COLS[:, c:c + 1], in1=f32(hi[:, 4 + g, :]),
                                                   op0=ALU.mult, op1=ALU.subtract)
                ins.then_inc(acc_read, 1)

            def halves(t, n):
                return [[x[:, j, TC:TA] for j in range(n)] for x in t], [[x[:, j, 0:TC] for j in range(n)] for x in t]

            inverse("cq")
            m, c = halves(CQ, 3)
            scaled("cq", LAT_M[0:3], LAT_C[0:3], m, c, gain_cols("g_q"), None)
            inverse("ckv")
            m, c = halves(CKV, 2)
            scaled("ckv", LAT_M[3:5], LAT_C[3:5], m, c, gain_cols("g_kv"), None)

            SWAP = [p ^ 1 for p in range(32)]

            def rope(n, rows, src, dst, done, table=ROPE_TA, rt=RT):
                dve.tensor_tensor(rt[0][rows], src, table[rows, 0, :], ALU.mult).then_inc(rope_step, 1)
                dve.stream_shuffle(rt[1][rows], src, SWAP).then_inc(rope_step, 1)
                dve.wait_ge(rope_step, n.times(3, 2))
                dve.tensor_tensor(rt[1][rows], rt[1][rows], table[rows, 1, :], ALU.mult).then_inc(rope_step, 1)
                dve.wait_ge(rope_step, n.times(3, 3))
                dve.tensor_tensor(dst, rt[0][rows], rt[1][rows], ALU.add).then_inc(rope_done, 1)

            dve.wait_ge(rope_loaded, 16)
            kr = slice(NOPE, DH_A)
            rope(At(0), kr, LAT_M[5][kr], LAT_M[5][kr], rope_done)
            dve.wait_ge(kr_hi, 1)
            for h in range(2):
                ins = low(KA[1][kr, h, :], LAT[kr, 5, :], KA[0][kr, h, :])
            ins.then_inc(rope_used, 1)

            def maxima(u, w, rows):
                dve.wait_ge(score_done, u.times(1, 1))
                n = len(rows)
                src = row(u)[:, 0:sum(rows)].rearrange("p (n k) -> p n k", n=n)
                dve.tensor_reduce(STAT[:, w.mod(2), 0:n], src, AX.X, ALU.max, negate=True).then_inc(max_ready, 1)

            def probs(u, w, rows):
                dve.wait_ge(score_free[u.mod(2)], u.over(2).times(1, 2))
                st, n = STAT[:, w.mod(2), :], len(rows)
                dve.reciprocal(st[:, 4:4 + n], st[:, 2:2 + n]).then_inc(recip_ready, 1)
                dve.wait_ge(recip_ready, w.times(1, 1))
                at = 0
                for m, width in enumerate(rows):
                    ins = dve.tensor_scalar(PROB[:, w.mod(2), at:at + width], PROB[:, w.mod(2), at:at + width], st[:, 4 + m:5 + m], None, ALU.mult)
                    at += width
                ins.then_inc(prob_ready, 1)

            def attend(units, maximum, prob, low_part, out_low, meanwhile=None):
                maximum(0)
                maximum(1)
                prob(0)
                if meanwhile:
                    meanwhile()
                before = last = None
                for n, (w, blocks, half) in enumerate(units):
                    if n + 1 < len(units):
                        prob(n + 1)
                    if n + 2 < len(units):
                        maximum(n + 2)
                    dve.wait_ge(pt_hi, w.times(1, 1))
                    low_part(n)
                    if before is not None:
                        out_low(before)
                    before, last = last, half
                for x in (before, last):
                    if x is not None:
                        out_low(x)

            dve.wait_ge(bias_stored, 16)
            with dve.Fori(0, 4) as i:
                s, u = At(TILES["mla"], 2, i), At(0, MLA_U, i)
                rows96 = slice(0, DH_A)
                for h in range(2):
                    q, p = u + h, At(h, 2, i)
                    dve.wait_ge(rope_used, p.times(1, 1))
                    dve.wait_ge(score_done, q.times(1, 1))
                    rope(p + 1, rows96, row(q)[rows96, TC:TA], RT[0][rows96], rope_done)
                    dve.wait_ge(proj_hi, At(h, 6, i).times(1, 1))
                    low(QA[1][rows96, h, 0:TC], row(q)[rows96, 0:TC], QA[0][rows96, h, 0:TC]).then_inc(score_free[q.mod(2)], 1)
                    dve.wait_ge(rope_done, p.times(1, 2))
                    low(QA[1][rows96, h, TC:TA], RT[0][rows96], QA[0][rows96, h, TC:TA]).then_inc(rope_used, 1)
                split(s + 2)
                for h in range(2):
                    k = u + 2 + h
                    dve.wait_ge(proj_hi, At(2 + h, 6, i).times(1, 1))
                    low(KA[1][0:NOPE, h, :], row(k)[0:NOPE, :], KA[0][0:NOPE, h, :]).then_inc(score_free[k.mod(2)], 1)
                for v in range(2):
                    uu = u + 4 + v
                    dve.wait_ge(proj_hi, At(4 + v, 6, i).times(1, 1))
                    low(VA[1][:, 3 * v:3 * v + 3, :], psf[:, uu.mod(2) * 1024:uu.mod(2) * 1024 + 3 * P].rearrange("p (b n) -> p b n", b=3),
                        VA[0][:, 3 * v:3 * v + 3, :]).then_inc(score_free[uu.mod(2)], 1)
                split(s + 3)
                mods(At(FIRST_MODS, MLA_MODS, i), MLA_MODS)
                w0, x0 = At(0, MLA_W, i), At(0, MLA_X, i)
                units = [(w0 + (5 * h + n), 4 if n == 0 else 6, None if n in (1, 3) else x0 + (3 * h + (n + 1) // 2))
                         for h in range(2) for n in range(5)]

                def widths(n):
                    return (TC, TC) if n % 5 == 0 else (TA,)

                def low_part(n):
                    x = x0 + (3 * (n // 5) + (n % 5 + 1) // 2)
                    dst, src = pt_views(n % 5, x, PTA[1])
                    hi, _ = pt_views(n % 5, x, PTA[0])
                    low(dst, src, hi).then_inc(pt_ready, 1)

                def out_low(x):
                    h, half = (x.start - x0.start) // 3, (x.start - x0.start) % 3
                    dve.wait_ge(o_hi, x.times(1, 1))
                    rows = slice(h * 64, h * 64 + 64)
                    hi, lo = [(g[rows, bass.ds(i, 1), :] if half == 0 else g[rows, bass.ds(i, 1), (half - 1) * 256:half * 256]
                               ).rearrange("p a n -> p (a n)") for g in (GC if half == 0 else GM)]
                    low(lo, out_half(x)[rows], hi).then_inc(o_read, 1)

                attend(units, lambda n: maxima(u + (6 + n), w0 + n, widths(n)), lambda n: probs(u + (6 + n), w0 + n, widths(n)),
                       low_part, out_low)

            def add_gated(u, layer, part, m, ctx_too):
                dve.wait_ge(acc_done, u.times(1, 1))
                dve.wait_ge(acc_read, u.times())
                col = m + (layer * 48 + part * 8)

                def update(x, src, v):
                    xx = x[:, m.ds(), :].rearrange("p a n -> p (a n)")
                    return dve.scalar_tensor_tensor(out=xx, in0=src, scalar=MOD[:, col.ds(), v:v + 1].rearrange("p a v -> p (a v)"), in1=xx,
                                                    op0=ALU.mult, op1=ALU.add)

                if ctx_too:
                    update(X_C, acc_ctx(u), 1)
                update(X_M, acc_main(u), 0).then_inc(acc_read, 1)

            def out_projection(tile, unit, layer, ctx_too):
                with dve.Fori(0, 2) as i:
                    for m in range(4):
                        add_gated(At(unit, 4, i) + m, layer, 2, At(m, 4, i), ctx_too)
                        split(At(tile + m + 2, 4, i))

            mods(At(FIRST_MODS + 4 * MLA_MODS), OUT_MODS)
            out_projection(TILES["mix_out"], UNIT["mix_out"], 0, True)

            def ffn(layer, ctx_too, n_mod, with_mods):
                name = f"ffn{layer}"
                scale1(n_mod, layer, 4)
                inverse(name, 0 if ctx_too else TC)
                scaled(name, X_CHUNKS, C_CHUNKS if ctx_too else None, both(HM), both(HC) if ctx_too else None,
                       scale1_gain, mod_shift(layer, 3))
                cols = COL[f"conv{layer}"]
                segs = ([(acc_ctx, 0, TC, GC)] if ctx_too else []) + [(acc_main, TC, TA, GM)]

                def group(i, n0, count, ahead=True):
                    s, u = At(TILES[name] + 3 * n0, 12, i), At(UNIT[name] + 4 * n0, 16, i)
                    f, fg = At(n0, 4, i), At(layer * FC + n0, 4, i)
                    for n in range(count):
                        sg, ug, fn, r = s + 2 * n, u + 2 * n, fg + n, (fg + n).mod(2)
                        split(sg + 2)
                        dve.wait_ge(conv_center, fn.times(1, 1))
                        for acc, b, e, _ in segs:
                            ins = dve.scalar_tensor_tensor(out=CONV[:, r, b + 1:e], in0=acc(ug)[:, 0:e - b - 1],
                                                           scalar=COLS[:, (f + n).ds(1, 1, cols)], in1=CONV[:, r, b + 1:e],
                                                           op0=ALU.mult, op1=ALU.add)
                        ins.then_inc(conv_tap, 1)
                        dve.wait_ge(conv_tap, fn.times(1, 1))
                        for acc, b, e, _ in segs:
                            ins = dve.scalar_tensor_tensor(out=CONV[:, r, b:e - 1], in0=acc(ug)[:, 1:e - b],
                                                           scalar=COLS[:, (f + n).ds(1, 1, cols + 2 * FC)], in1=CONV[:, r, b:e - 1],
                                                           op0=ALU.mult, op1=ALU.add)
                        ins.then_inc(acc_read, 1)
                        if with_mods:
                            pair = At((FIRST_MODS + 4 * MLA_MODS + OUT_MODS) // 2 + n0 + n, 4, i)
                            mod_take(pair)
                        split(sg + 3)
                        dve.wait_ge(silu_done, fn.times(1, 1))
                        for acc, b, e, _ in segs:
                            ins = dve.tensor_tensor(GATED[:, r, b:e], CONV[:, r, b:e], acc(ug + 1), ALU.mult)
                        ins.then_inc(acc_read, 1)
                        if with_mods:
                            mod_add(pair)
                        dve.wait_ge(gated_hi, fn.times(1, 1))
                        for acc, b, e, g in segs:
                            ins = low(g[1][:, n, :], GATED[:, r, b:e], g[0][:, n, :])
                        ins.then_inc(gated_ready, 1)
                    s, u = s + 2 * count, u + 2 * count
                    per_tile = KC // count
                    for m in range(KC):
                        add_gated(u + m, layer, 5, At(m), ctx_too)
                        if ahead and (m + 1) % per_tile == 0:
                            split(s + m // per_tile + 2)

                with dve.Fori(0, 5) as i:
                    group(i, 0, 4)
                group(None, 20, 2, layer == 0)

            ffn(0, True, 1, True)

            def head_norm(m, u, gain, lo):
                sq = SQ[:, m.mod(2), lo:TA]
                dve.wait_ge(head_rms, m.times(1, 1))
                dve.reciprocal(sq, sq).then_inc(head_inverse, 1)
                dve.wait_ge(head_inverse, m.times(1, 1))
                if m.i is not None or m.start >= 2:
                    dve.wait_ge(head_split, (m - 1).times())
                dve.scalar_tensor_tensor(out=HEADN[:, m.mod(2), lo:TA], in0=row(u)[:, lo:TA], scalar=COLS[:, COL[gain]:COL[gain] + 1], in1=sq,
                                         op0=ALU.mult, op1=ALU.mult).then_inc(score_free[u.mod(2)], 1)

            def rotated(m, u):
                dve.wait_ge(score_free[u.mod(2)], u.over(2).times(1, 2))
                if m.i is not None or m.start:
                    dve.wait_ge(head_split, m.times())
                rope(m + 9, slice(0, P), HEADN[:, m.mod(2), TC:TA], RG[0][:, :], rope_done, ROPE_TG, RG)

            scale1(2, 1, 1)
            inverse("mix1")
            scaled("mix1", X_CHUNKS, C_CHUNKS, both(HM), both(HC), scale1_gain, mod_shift(1, 0))
            s, u = At(TILES["gqa_kv"]), At(4 * MLA_U)
            for n in range(2):
                split(s + 2 + n)
            dve.wait_ge(norm_ready, SPLITS["ffn1"])
            dve.wait_ge(rope_c_loaded, 16)
            for n in range(2):
                head_norm(At(n), u + n, "gk", 0)
            for n in range(2):
                rotated(At(n), u + n)
                dve.wait_ge(proj_hi, 24 + n + 1)
                low(KG[1][:, n, 0:TC], HEADN[:, n, 0:TC], KG[0][:, n, 0:TC])
                low(KG[1][:, n, TC:TA], RG[0][:, :], KG[0][:, n, TC:TA]).then_inc(head_split, 1)
            for v in range(4):
                uu = u + 2 + v
                dve.wait_ge(proj_hi, 26 + v + 1)
                b = 3 * (v % 2)
                low(VG[1][:, b:b + 3, v // 2, :], psf[:, uu.mod(2) * 1024:uu.mod(2) * 1024 + 3 * P].rearrange("p (b n) -> p b n", b=3),
                    VG[0][:, b:b + 3, v // 2, :]).then_inc(score_free[uu.mod(2)], 1)
                if v % 2:
                    split(s + 4 + v // 2)
            for kv in range(2):
                with dve.Fori(0, 2) as i:
                    s, u = At(TILES["gqa_q"] + 4 * kv, 2, i), At(GQA_Q + 2 * GQA_U * kv, GQA_U, i)
                    w0 = At(4 * MLA_W + 2 * GQA_W * kv, GQA_W, i)
                    x0 = At(4 * MLA_X + 2 * GQA_X * kv, GQA_X, i)
                    m = At(2 + 4 * kv, 2, i)
                    def query(h):
                        rotated(m + h, u + h)
                        dve.wait_ge(proj_hi, (m + h).times(1, 29))
                        low(QG[1][:, h, :], RG[0][:, :], QG[0][:, h, :]).then_inc(head_split, 1)

                    head_norm(m, u, "gq", TC)
                    query(0)
                    head_norm(m + 1, u + 1, "gq", TC)

                    def meanwhile():
                        query(1)
                        split(s + 2)
                        split(s + 3)

                    def low_part(n):
                        x = x0 + n // 2
                        dst, src = pt_views(n % 4 + 1, x, PTG[1])
                        hi, _ = pt_views(n % 4 + 1, x, PTG[0])
                        low(dst, src, hi).then_inc(pt_ready, 1)

                    def out_low(x):
                        h, half = (x.start - x0.start) // 2, (x.start - x0.start) % 2
                        dve.wait_ge(o_hi, x.times(1, 1))
                        hi, lo = [g[:, At(4 * kv + h, 2, i).ds(), half * 256:half * 256 + 256].rearrange("p a n -> p (a n)") for g in GM]
                        low(lo, out_half(x), hi).then_inc(o_read, 1)

                    attend([(w0 + n, 6, None if n % 2 == 0 else x0 + n // 2) for n in range(8)],
                           lambda n: maxima(u + (2 + n), w0 + n, (TA,)), lambda n: probs(u + (2 + n), w0 + n, (TA,)), low_part, out_low, meanwhile)
            out_projection(TILES["gqa_out"], UNIT["gqa_out"], 1, False)
            ffn(1, False, 3, False)

            def post_norm(name, n_before, src, gain, dst, view=lambda x: x):
                inverse(name, TC)
                for j in range(KC):
                    dve.scalar_tensor_tensor(out=src[j], in0=src[j], scalar=gain(j, 0), in1=RB[:, TC:TA], op0=ALU.mult, op1=ALU.mult
                                             ).then_inc(post_scaled, 1)
                    if j:
                        dve.wait_ge(post_scaled, n_before + j)
                        dve.tensor_tensor(dst[j - 1], dst[j - 1], view(src[j - 1]), ALU.add).then_inc(x_ready, 1)
                dve.wait_ge(post_scaled, n_before + KC)
                dve.tensor_tensor(dst[KC - 1], dst[KC - 1], view(src[KC - 1]), ALU.add).then_inc(x_ready, 1)

            for n in range(2):
                t = At(TILES["ws"] + n)
                dve.wait_ge(tile_hi, t.times(1, 1))
                low(WS[1][:, n * D:(n + 1) * D], RAW[:, t.mod(2), :], WS[0][:, n * D:(n + 1) * D]).then_inc(tile_split[t.mod(2)], 1)
            inverse("final", TC)
            for j in range(KC):
                dve.scalar_tensor_tensor(out=X_CHUNKS[j], in0=X_CHUNKS[j], scalar=gain_cols("g_final")(j, 0), in1=RB[:, TC:TA],
                                         op0=ALU.mult, op1=ALU.mult).then_inc(x_ready, 1)
            s = At(TILES["gmlp_v"])
            split(s)
            split(s + 1)
            inverse("gmlp", TC)
            scaled("gmlp", X_CHUNKS, None, both(HM), None, gain_cols("pre0"), None)
            with dve.Fori(0, 2) as i:
                for g in range(2):
                    for t in range(4):
                        split(At(TILES["gmlp_v"] + 4 * g + t + 2, 8, i))
            dve.wait_ge(acc_read, UNIT["gmlp"])
            dve.tensor_reduce(LN[:, 1, 4:8], LN[:, 0, 0:16].rearrange("p (g b) -> p b g", g=4), AX.X, ALU.add, negate=True).then_inc(mean_ready, 1)
            dve.wait_ge(mean_ready, 1)
            dve.tensor_scalar(LN[:, 1, 0:4], LN[:, 1, 4:8], 1.0 / (A_HEADS * P), None, ALU.mult).then_inc(mean_ready, 1)
            dve.wait_ge(std_ready, 1)
            dve.reciprocal(LN[:, 3, 4:8], LN[:, 3, 0:4]).then_inc(std_ready, 1)
            dve.wait_ge(std_ready, 2)
            for b in range(4):
                ins = dve.tensor_scalar(V[:, b, :], V[:, b, :], LN[:, 1, b:b + 1], LN[:, 3, 4 + b:5 + b], ALU.add, ALU.mult)
            ins.then_inc(v_normed, 1)
            dve.wait_ge(v_normed, 1)
            dve.wait_ge(rows_loaded, 48)
            dve.wait_ge(y_zero, 1)
            with dve.Fori(0, 4) as i:
                s, u, f = At(TILES["gmlp"], 12, i), At(UNIT["gmlp"], 20, i), At(0, 4, i)
                for h in range(4):
                    t, uu, fh = s + 2 * h, u + 3 * h, f + h
                    cols_h = bass.ds(fh.times(P), P)

                    def spread(row_):
                        return row_.unsqueeze(1).to_broadcast([P, 4, P])

                    dve.wait_ge(vs_ready, fh.times(1, 1))
                    dve.tensor_tensor(VT[:, :, :], V[:, :, cols_h], spread(VN_GB[:, 0, cols_h]), ALU.mult).then_inc(v_step, 1)
                    dve.wait_ge(v_step, fh.times(2, 1))
                    dve.tensor_tensor(VT[:, :, :], VT[:, :, :], spread(VN_GB[:, 1, cols_h]), ALU.add).then_inc(v_step, 1)
                    split(t + 2)
                    dve.wait_ge(vs_hi, fh.times(1, 1))
                    low(VS[1][:, :, :], VT[:, :, :], VS[0][:, :, :]).then_inc(vs_ready, 1)
                    split(t + 3)
                    dve.wait_ge(th_ready, fh.times(1, 1))
                    dve.wait_ge(y_ready, fh.times(1, 1))
                    dve.scalar_tensor_tensor(out=GG[:, :], in0=TH[:, :], scalar=1.0, in1=acc_main(uu + 1), op0=ALU.add, op1=ALU.mult
                                             ).then_inc(acc_read, 1)
                    dve.wait_ge(acc_read, uu.times(1, 2))
                    dve.tensor_tensor(GG[:, :], GG[:, :], UG[:, :], ALU.mult).then_inc(gu_ready, 1)
                    dve.wait_ge(acc_done, uu.times(1, 3))
                    dve.tensor_tensor(SB[:, :].rearrange("p (b n) -> p b n", b=4), acc_main(uu + 2).rearrange("p (b n) -> p b n", b=4),
                                      spread(BS[:, cols_h]), ALU.add).then_inc(acc_read, 1)
                    dve.wait_ge(gu_ready, fh.times(1, 1))
                    dve.wait_ge(acc_read, uu.times(1, 3))
                    dve.wait_ge(gm_ready, fh.times(1, 1))
                    dve.scalar_tensor_tensor(out=YG[:, :], in0=SB[:, :], scalar=0.5, in1=GG[:, :], op0=ALU.mult, op1=ALU.mult
                                             ).then_inc(y_ready, 1)
                    dve.wait_ge(gm_hi, fh.times(1, 1))
                    low(PG[1][:, h, :], YG[:, :], PG[0][:, h, :]).then_inc(gm_ready, 1)
                for m in range(KC):
                    um = u + (12 + m)
                    dve.wait_ge(acc_done, um.times(1, 1))
                    dve.wait_ge(acc_read, um.times())
                    dve.tensor_tensor(Y[:, m, :], Y[:, m, :], acc_main(um), ALU.add).then_inc(acc_read, 1)
                    if m % 2:
                        split(s + (10 + m // 2))
            post_norm("gmlp_post", 0, chunks(Y), gain_cols("post0"), X_CHUNKS)

            def by_residue(t):
                return t.rearrange("p (l r) -> p r l", r=4)

            inverse("dil", TC)
            scaled("dil", X_CHUNKS, None, both(HM), None, gain_cols("pre1"), None, True)
            with dve.Fori(0, 8) as i:
                s, u = At(TILES["dil"], 10, i), At(DIL_U0, DIL_U, i)
                w0, x0 = At(DIL_W0, DIL_W, i), At(DIL_X0, DIL_X, i)
                order = 0
                for n in range(10):
                    t, uu = s + n, u + n
                    src = row(uu)[:, TC:TA]
                    if n == 3:
                        dve.wait_ge(thg_ready, At(0, 1, i).times(1, 1))
                        dve.wait_ge(o_read, x0.times(1, 2))
                        dve.scalar_tensor_tensor(out=SILG[:, :], in0=THG[:, :], scalar=1.0, in1=src, op0=ALU.add, op1=ALU.mult
                                                 ).then_inc(score_free[uu.mod(2)], 1)
                    elif n > 3:
                        g, is_k = (n - 4) // 2, n % 2
                        order += 1
                        dve.wait_ge(dil_hi, At(0, 9, i).times(1, order))
                        if is_k:
                            ins = low(forwards(KD[1][:, g, :]), backwards(src), forwards(KD[0][:, g, :]))
                        else:
                            ins = dve.scalar_tensor_tensor(out=QD[1][:, g, :], in0=src, scalar=0.125, in1=f32(QD[0][:, g, :]),
                                                           op0=ALU.mult, op1=ALU.subtract)
                        ins.then_inc(score_free[uu.mod(2)], 1)
                    split(t + 2)
                    if n in (4, 5):
                        for g in (0, 1) if n == 4 else (2,):
                            order += 1
                            dve.wait_ge(dil_hi, At(0, 9, i).times(1, order))
                            low(VD[1][:, g, :, :].rearrange("p b n -> p (b n)"), PS[:, 4 + g % 2, :],
                                VD[0][:, g, :, :].rearrange("p b n -> p (b n)")).then_inc(vt_read, 1)

                def maximum(n):
                    uu, w, h, r, at = u + (10 + n), w0 + n, n // 4, n % 4, At(n, DIL_W, i)
                    st = STAT[:, w.mod(2), :]
                    if r == 0:
                        dve.wait_ge(tb_loaded[h], At(0, 1, i).times(16, 16))
                    dve.wait_ge(score_done, uu.times(1, 1))
                    dve.wait_ge(pt_done, w.times(1, -3))
                    dve.tensor_tensor(PROB4[:, w.mod(4), 0:TC].rearrange("p (b n) -> p b n", b=2),
                                      row(uu)[:, 0:TC].rearrange("p (b n) -> p b n", b=2), TB[:, h, 0:2, :], ALU.add)
                    dve.tensor_tensor(PROB4[:, w.mod(4), TC:TA].rearrange("p (b n) -> p b n", b=4),
                                      row(uu)[:, TC:TA].rearrange("p (b n) -> p b n", b=4), TB[:, h, 5 - r:9 - r, :], ALU.add
                                      ).then_inc(score_free[uu.mod(2)], 1)
                    dve.wait_ge(score_free[uu.mod(2)], uu.over(2).times(1, 2))
                    dve.tensor_reduce(st[:, 0:1], PROB4[:, w.mod(4), :], AX.X, ALU.max, negate=True).then_inc(both_max, 1)

                def prob(n):
                    w = w0 + n
                    st = STAT[:, w.mod(2), :]
                    dve.wait_ge(exp_ready, At(n, DIL_W, i).times(1, 1))
                    dve.reciprocal(st[:, 4:5], st[:, 2:3]).then_inc(recip_ready, 1)
                    dve.wait_ge(recip_ready, w.times(1, 1))
                    dve.tensor_scalar(PROB4[:, w.mod(4), :], PROB4[:, w.mod(4), :], st[:, 4:5], None, ALU.mult).then_inc(prob_ready, 1)

                def low_part(n):
                    x = x0 + n // 2
                    dst, src = pt_views(n % 4 + 1, x, PTD[1])
                    hi, _ = pt_views(n % 4 + 1, x, PTD[0])
                    low(dst, src, hi).then_inc(pt_ready, 1)

                def out_low(x):
                    h, half = (x.start - x0.start) // 2, (x.start - x0.start) % 2
                    rows, cols = slice(h * 64, h * 64 + 64), slice(half * 256, half * 256 + 256)
                    dve.wait_ge(o_done, x.times(1, 3))
                    dve.wait_ge(o_read, x.times(1, 2))
                    dve.scalar_tensor_tensor(out=OG[rows, :], in0=out_half(x)[rows], scalar=0.5, in1=SILG[rows, cols], op0=ALU.mult, op1=ALU.mult
                                             ).then_inc(o_scaled, 1)
                    dve.wait_ge(o_hi, x.times(1, 1))
                    hi, lo = [g[rows, bass.ds(i, 1), cols].rearrange("p a n -> p (a n)") for g in DG]
                    low(lo, OG[rows, :], hi).then_inc(o_read, 1)

                attend([(w0 + n, 6, None if n % 2 == 0 else x0 + n // 2) for n in range(8)], maximum, prob, low_part, out_low)
            for m in range(KC):
                um = At(UNIT["dil_out"]) + m
                dve.wait_ge(acc_done, um.times(1, 1))
                dve.tensor_copy(YD[:, m, :], acc_main(um)).then_inc(acc_read, 1)
                if m < KC - 2:
                    split(At(TILES["dil_out"] + m + 2))
            dve.wait_ge(acc_read, UNIT["dil_out"] + KC)
            post_norm("dil_post", KC, chunks(YD), gain_cols("post1"), [by_residue(x) for x in X_CHUNKS], lambda y: y.rearrange("p (r l) -> p r l", r=4))


def columns(v):
    return np.ascontiguousarray(np.asarray(v).reshape(-1, P).T)


def k_tiles(w, c, n=P):
    k = w.shape[0] // P
    return w[:, c:c + n].reshape(k, P, n).transpose(1, 0, 2).reshape(P, k * n)


def padded(*parts):
    t = np.zeros((P, D), np.float32)
    at = 0
    for p in parts:
        t[:, at:at + p.shape[1]] = p
        at += p.shape[1]
    return t


def ffn_tiles(up, down):
    out = []
    for g in range(0, FC, GROUP):
        n = min(GROUP, FC - g)
        for f in range(g, g + n):
            out += [k_tiles(up, f * P), k_tiles(up, FF + f * P)]
        per = D // n
        for c in range(0, D, per):
            out.append(k_tiles(down[g * P:(g + n) * P], c, per))
    return out


def pack_tiles(v):
    t = []
    w = v["mix0_w_in"][0]
    i_kr = Q_RANK + KV_RANK
    i_p = i_kr + ROPE_A
    t += [k_tiles(w, i_p + g * P) for g in range(4)]
    t += [k_tiles(w, c) for c in range(0, i_kr, P)]
    kr = np.zeros((D, P), np.float32)
    kr[:, NOPE:DH_A] = w[:, i_kr:i_p]
    t.append(k_tiles(kr, 0))
    t.append(padded(*[v["pool_w"][0, g] for g in range(4)]))
    for i in range(4):
        t.append(padded(k_tiles(v["mla_w_uq"][0], i * 2 * DH_A, 2 * DH_A)))
        t.append(padded(k_tiles(v["mla_w_uk"][0], i * P), k_tiles(v["mla_w_uv"][0], i * P)))
    t += [k_tiles(v["mix0_w_out"][0], m * P) for m in range(8)]
    t += ffn_tiles(v["ffn_w_up"][0], v["ffn_w_down"][0])
    w = v["gqa_w_in"][0]
    t += [k_tiles(w, D + n * P) for n in range(4)] + [k_tiles(w, h * P) for h in range(8)]
    t += [k_tiles(v["gqa_w_out"][0], m * P) for m in range(8)]
    t += ffn_tiles(v["ffn_w_up"][1], v["ffn_w_down"][1])
    ws = v["a_w_s_2"][0].transpose(2, 0, 1)
    t += [ws[:, n * 8:(n + 1) * 8].reshape(P, D) for n in range(2)]
    w, wo = v["a_w_in_2"][0], v["a_w_out_2"][0]
    for g in range(4):
        t += [k_tiles(w[k * 2 * P:(k + 1) * 2 * P], 2048 + g * 512, 512) for k in range(4)]
    for g in range(4):
        for h in range(4 * g, 4 * g + 4):
            t += [k_tiles(w, h * P), k_tiles(w, 4096 + h * P)]
        t += [k_tiles(wo[g * 512:(g + 1) * 512], c, 256) for c in range(0, D, 256)]
    w = v["b_w_in_2"][0]
    for i in range(8):
        q = [g * 3 * D + i * P for g in range(3)]
        for c in (q[0] + 2 * D, q[1] + 2 * D, q[2] + 2 * D, 9 * D + i * P, q[0], q[0] + D, q[1], q[1] + D, q[2], q[2] + D):
            t.append(k_tiles(w, c))
    t += [k_tiles(v["b_w_out_2"][0], m * P) for m in range(8)]
    assert len(t) == N_TILES, (len(t), N_TILES)
    return np.stack(t)


def rope_tables(dim, rows_before):
    n_freq = dim // 4
    freq = np.float32(10000.0) ** (-np.arange(n_freq, dtype=np.float32) / np.float32(n_freq))
    row_, col_ = np.divmod(np.arange(TM), GRID_W)
    ang = np.concatenate([row_[:, None].astype(np.float32) * freq, col_[:, None].astype(np.float32) * freq], -1)
    t = np.zeros((P, 2, TM), np.float32)
    t[:rows_before, 0] = 1
    n = slice(rows_before, rows_before + dim)
    t[n, 0] = np.repeat(np.cos(ang).T, 2, 0)
    t[n, 1] = np.repeat(np.sin(ang).T, 2, 0) * np.tile([-1, 1], dim // 2)[:, None]
    return t


def edge_factors():
    t = np.zeros((4, 4, PAD), np.float32)
    for g, w in enumerate(WINDOWS):
        for seg, n in enumerate((TC, TM)):
            i = np.arange(n)
            f = w / (np.clip(i - w // 2 + w, 0, n) - np.clip(i - w // 2, 0, n))
            t[g, 2 * seg], t[g, 2 * seg + 1] = f[:PAD], f[-PAD:]
    return np.ascontiguousarray(np.broadcast_to(t, (P, 4, 4, PAD)))


def bias_rows():
    onehot = np.zeros((BUCKETS, NREL, TW), np.float32)
    mask = np.full((NREL, TW), NEG, np.float32)
    half, exact = BUCKETS // 2, 8
    for r in range(NREL):
        for t in range(TW - 1):
            d = P - 1 - t
            if r == 0:
                rel, ok = 4 * d, abs(d) <= HALF_W
            elif r == 1:
                rel, ok = 4 * d, d % 4 == 0
            else:
                rel = 4 * d + r - 2 - 3
                ok = abs(rel) <= HALF_W
            if ok:
                n = abs(rel)
                b = n if n < exact else min(exact + int(np.log(n / exact) / np.log(1024 / exact) * (half - exact)), half - 1)
                onehot[b + (half if rel > 0 else 0), r, t] = 1
                mask[r, t] = 0
    return onehot.reshape(BUCKETS, -1), np.ascontiguousarray(np.broadcast_to(mask.reshape(-1), (B_HEADS, NREL * TW)))


def device_arrays(v):
    cols = [columns(v["b_mod"]), columns(v["mla_g_q"][0]), columns(v["mla_g_kv"][0]), columns(v["pool_scale"][0]),
            columns(v["gqa_g_q"][0]), columns(v["gqa_g_k"][0])]
    for l in range(2):
        cols += [columns(v["ffn_conv_w"][l]), columns(v["ffn_conv_b"][l])]
    cols += [columns(v["g_final"]), columns(v["norm_pre_2"]), columns(v["norm_post_2"])]
    return {
        "tiles": pack_tiles(v),
        "mods": v["w_mod"].reshape(2, KC, P, 48, P).transpose(0, 3, 2, 1, 4).reshape(96, P, D),
        "x": v["x"][0].T.reshape(KC, P, TM).transpose(1, 0, 2),
        "ctx": v["ctx"][0].T.reshape(KC, P, TC).transpose(1, 0, 2),
        "cvec": np.stack([columns(v["c"][0]), columns(v["c_ctx"])], -1),
        "cols": np.concatenate(cols, 1),
        "ident": np.eye(P, dtype=np.float32),
        "edge": edge_factors(),
        "gm_rows": np.stack([v["a_vnorm_g_2"][0], v["a_vnorm_b_2"][0], v["a_b_s_2"][0].reshape(-1)]),
        "rel": v["rel_bias_2"],
        "onehot": bias_rows()[0],
        "relmask": bias_rows()[1],
        "rope_a": rope_tables(ROPE_A, NOPE),
        "rope_c": rope_tables(P, 0),
    }


def kernel(**inputs):
    import concourse.bacc as bacc
    from concourse.bass_utils import run_bass_kernel_spmd

    v = {n: np.asarray(x) for n, x in inputs.items()}
    nc = bacc.Bacc("TRN2", target_bir_lowering=False, num_devices=1)
    arrays, aps = {}, {}
    for name, x in device_arrays(v).items():
        arrays[f"in_{name}"] = np.ascontiguousarray(x)
        aps[name] = nc.dram_tensor(f"in_{name}", x.shape, F32, kind="ExternalInput").ap()
    out = nc.dram_tensor("out_x", (P, KC, TM), F32, kind="ExternalOutput").ap()
    build(nc, aps, out)
    r = run_bass_kernel_spmd(nc, [arrays], core_ids=[0])
    return np.asarray(r.results[0]["out_x"]).transpose(1, 0, 2).reshape(D, TM).T[None]
```
